# Optimizing a Trainium2 kernel written in Bass

```python
import jax, jax.numpy as jnp
from jax import lax
import numpy as np

D_MODEL = 1024
BATCH = 1
SEQ = 1024
DEPTH = 1

CHUNK = 64
PLE_DIM = 256
EPS = 1e-6
LRU_WIDTH = D_MODEL // 2
LRU_BLOCKS = 8
LRU_BLOCK = LRU_WIDTH // LRU_BLOCKS
CONV_WIDTH = 4
LRU_C = 8.0
N_Q_HEADS = 8
N_KV_HEADS = 2
HEAD_DIM = 64
Q_GROUP = N_Q_HEADS // N_KV_HEADS
WINDOW = 128
WINDOW_CHUNKS = WINDOW // CHUNK
ATTN_WIDTH = N_Q_HEADS * HEAD_DIM
KV_WIDTH = N_KV_HEADS * HEAD_DIM
MIX_WIDTH = LRU_WIDTH + ATTN_WIDTH
IN_WIDTH = 2 * LRU_WIDTH + ATTN_WIDTH + 2 * KV_WIDTH
D_FF = 4 * D_MODEL
NEG_INF = -1e30

kernel_name = "hymba_rglru_swa_sink_alibi_block"

def rmsnorm(x, g):
    xf = x.astype(jnp.float32)
    y = xf * lax.rsqrt(jnp.mean(xf * xf, axis=-1, keepdims=True) + EPS)
    return (y * g.astype(jnp.float32)).astype(x.dtype)

def causal_depthwise_conv(x, w, b):
    s = x.shape[1]
    xp = jnp.pad(x, ((0, 0), (CONV_WIDTH - 1, 0), (0, 0)))
    out = b
    for k in range(CONV_WIDTH):
        out = out + xp[:, k:k + s] * w[k]
    return out

def _lin_rec_combine(e1, e2):
    a1, b1 = e1
    a2, b2 = e2
    return a1 * a2, a2 * b1 + b2

def rg_lru(x, w_a, b_a, w_i, b_i, lam):
    bsz, s, _ = x.shape
    xb = x.reshape(bsz, s, LRU_BLOCKS, LRU_BLOCK)
    r = jax.nn.sigmoid((jnp.einsum('bsnc,ncd->bsnd', xb, w_a).reshape(bsz, s, LRU_WIDTH) + b_a).astype(jnp.float32))
    ig = jax.nn.sigmoid((jnp.einsum('bsnc,ncd->bsnd', xb, w_i).reshape(bsz, s, LRU_WIDTH) + b_i).astype(jnp.float32))
    log_a = LRU_C * r * jax.nn.log_sigmoid(lam.astype(jnp.float32))
    a = jnp.exp(log_a)
    mult = jnp.sqrt(-jnp.expm1(2.0 * log_a))
    bterm = mult * (ig * x.astype(jnp.float32))
    _, h = lax.associative_scan(_lin_rec_combine, (a, bterm), axis=1)
    return h.astype(x.dtype)

def alibi_slopes(n_heads):
    return jnp.power(2.0, -8.0 * jnp.arange(1, n_heads + 1, dtype=jnp.float32) / n_heads)

def chunk_window_attention(q, k, v, sinks):
    bsz, s = q.shape[:2]
    nc = s // CHUNK
    pad = (WINDOW_CHUNKS - 1) * CHUNK
    kw = WINDOW_CHUNKS * CHUNK
    qc = q.reshape(bsz, nc, CHUNK, N_KV_HEADS, Q_GROUP, HEAD_DIM)
    kp = jnp.pad(k, ((0, 0), (pad, 0), (0, 0), (0, 0))).reshape(bsz, nc + WINDOW_CHUNKS - 1, CHUNK, N_KV_HEADS, HEAD_DIM)
    vp = jnp.pad(v, ((0, 0), (pad, 0), (0, 0), (0, 0))).reshape(bsz, nc + WINDOW_CHUNKS - 1, CHUNK, N_KV_HEADS, HEAD_DIM)
    kb = jnp.concatenate([kp[:, w:w + nc] for w in range(WINDOW_CHUNKS)], axis=2)
    vb = jnp.concatenate([vp[:, w:w + nc] for w in range(WINDOW_CHUNKS)], axis=2)
    scores = jnp.einsum('bcqhgd,bckhd->bhgcqk', qc, kb,
                        preferred_element_type=jnp.float32) * (HEAD_DIM ** -0.5)
    qi = jnp.arange(CHUNK)
    kj = jnp.arange(kw)
    dist = jnp.abs(pad + qi[:, None] - kj[None, :]).astype(jnp.float32)
    slopes = alibi_slopes(N_Q_HEADS).reshape(N_KV_HEADS, Q_GROUP)
    bias = -slopes[:, :, None, None, None] * dist[None, None, None]
    key_pos = jnp.arange(nc)[:, None] * CHUNK - pad + kj[None, :]
    valid = (key_pos >= 0)[None, None, None, :, None, :]
    scores = jnp.where(valid, scores + bias[None], NEG_INF)
    sink = jnp.broadcast_to(sinks.astype(jnp.float32).reshape(1, N_KV_HEADS, Q_GROUP, 1, 1, 1),
                            scores.shape[:-1] + (1,))
    probs = jax.nn.softmax(jnp.concatenate([scores, sink], axis=-1), axis=-1)[..., :kw]
    out = jnp.einsum('bhgcqk,bckhd->bcqhgd', probs.astype(v.dtype), vb)
    return out.reshape(bsz, s, ATTN_WIDTH)

def setup_inputs(seed: int = 0) -> dict:
    key = jax.random.key(seed)
    ks = jax.random.split(key, 24)
    f32 = jnp.float32

    def nrm(k, shape, scale):
        return jax.random.normal(k, shape, f32) * scale

    def gain(k, shape):
        return 1.0 + 0.05 * jax.random.normal(k, shape, f32)

    a0 = jax.random.uniform(ks[10], (DEPTH, LRU_WIDTH), f32, 0.9, 0.999)
    base = a0 ** (1.0 / LRU_C)
    lam = jnp.log(base) - jnp.log1p(-base)
    return {
        "x": nrm(ks[0], (BATCH, SEQ, D_MODEL), 1.0),
        "p": nrm(ks[1], (DEPTH, BATCH, SEQ, PLE_DIM), 1.0),
        "g_mix": gain(ks[2], (DEPTH, D_MODEL)),
        "w_in": nrm(ks[3], (DEPTH, D_MODEL, IN_WIDTH), D_MODEL ** -0.5),
        "w_conv": nrm(ks[4], (DEPTH, CONV_WIDTH, LRU_WIDTH), CONV_WIDTH ** -0.5),
        "b_conv": nrm(ks[5], (DEPTH, LRU_WIDTH), 0.02),
        "w_lru_a": nrm(ks[6], (DEPTH, LRU_BLOCKS, LRU_BLOCK, LRU_BLOCK), LRU_BLOCK ** -0.5),
        "b_lru_a": nrm(ks[7], (DEPTH, LRU_WIDTH), 0.02),
        "w_lru_i": nrm(ks[8], (DEPTH, LRU_BLOCKS, LRU_BLOCK, LRU_BLOCK), LRU_BLOCK ** -0.5),
        "b_lru_i": nrm(ks[9], (DEPTH, LRU_WIDTH), 0.02),
        "lru_lambda": lam,
        "sinks": nrm(ks[11], (DEPTH, N_Q_HEADS), 0.5),
        "g_lru_out": gain(ks[12], (DEPTH, LRU_WIDTH)),
        "g_attn_out": gain(ks[13], (DEPTH, ATTN_WIDTH)),
        "w_out": nrm(ks[14], (DEPTH, MIX_WIDTH, D_MODEL), MIX_WIDTH ** -0.5),
        "g_ffn": gain(ks[15], (DEPTH, D_MODEL)),
        "w_ff1": nrm(ks[16], (DEPTH, D_MODEL, D_FF), D_MODEL ** -0.5),
        "w_ff2": nrm(ks[17], (DEPTH, D_FF, D_MODEL), D_FF ** -0.5),
        "g_ple": gain(ks[18], (DEPTH, D_MODEL)),
        "w_ple_gate": nrm(ks[19], (DEPTH, D_MODEL, D_MODEL), D_MODEL ** -0.5),
        "w_ple_proj": nrm(ks[20], (DEPTH, PLE_DIM, D_MODEL), PLE_DIM ** -0.5),
        "g_final": gain(ks[21], (D_MODEL,)),
    }

def reference(x, p, g_mix, w_in, w_conv, b_conv, w_lru_a, b_lru_a, w_lru_i, b_lru_i,
              lru_lambda, sinks, g_lru_out, g_attn_out, w_out, g_ffn, w_ff1, w_ff2,
              g_ple, w_ple_gate, w_ple_proj, g_final):
    bsz, s, _ = x.shape
    o1 = LRU_WIDTH
    o2 = 2 * LRU_WIDTH
    o3 = o2 + ATTN_WIDTH
    o4 = o3 + KV_WIDTH
    for i in range(DEPTH):
        h = rmsnorm(x, g_mix[i])
        z = h @ w_in[i]
        lx, lg = z[..., :o1], z[..., o1:o2]
        q = z[..., o2:o3].reshape(bsz, s, N_Q_HEADS, HEAD_DIM)
        k = z[..., o3:o4].reshape(bsz, s, N_KV_HEADS, HEAD_DIM)
        v = z[..., o4:].reshape(bsz, s, N_KV_HEADS, HEAD_DIM)
        lx = causal_depthwise_conv(lx, w_conv[i], b_conv[i])
        y_lru = rg_lru(lx, w_lru_a[i], b_lru_a[i], w_lru_i[i], b_lru_i[i], lru_lambda[i])
        y_lru = rmsnorm(y_lru * jax.nn.gelu(lg), g_lru_out[i])
        y_att = rmsnorm(chunk_window_attention(q, k, v, sinks[i]), g_attn_out[i])
        x = x + jnp.concatenate([y_lru, y_att], axis=-1) @ w_out[i]
        h = rmsnorm(x, g_ffn[i])
        x = x + jnp.square(jax.nn.relu(h @ w_ff1[i])) @ w_ff2[i]
        gate = jax.nn.sigmoid(rmsnorm(x, g_ple[i]) @ w_ple_gate[i])
        x = x + gate * (p[i] @ w_ple_proj[i])
    return rmsnorm(x, g_final)


_drawn_inputs = setup_inputs


def setup_inputs(seed=0):
    import zlib

    import numpy as np

    out = dict(_drawn_inputs(seed))
    spreads = {}
    factors = {'b_lru_a': 21.369, 'b_lru_i': 8.0, 'g_ple': 25.929}
    for name, (base, spread) in spreads.items():
        noise = np.random.default_rng([zlib.crc32(name.encode()), seed]).standard_normal(out[name].shape)
        drawn = base * np.exp(spread * noise) if base else spread * noise
        out[name] = __import__('jax').numpy.asarray(drawn.astype(out[name].dtype))
    for name, factor in factors.items():
        out[name] = (out[name] * factor).astype(out[name].dtype)
    return out
```

```python
from contextlib import ExitStack

import numpy as np

import concourse.bass as bass
from concourse import mybir

F32 = mybir.dt.float32
F32R = mybir.dt.float32r
ALU = mybir.AluOpType
ACT = mybir.ActivationFunctionType
AX = mybir.AxisListType

P = 128
SEQ = 1024
D = 1024
KD = D // P
HALF = SEQ // 2
TT = SEQ // P
LRU = D // 2
LT = LRU // P
ATT = D // 2
HD = 64
NQ, NKV = 8, 2
CHUNK = 64
KVW = NKV * HD
IN_W = 2 * LRU + ATT + 2 * KVW
FF = 4 * D
PLE = 256
EPS = 1e-6
NEG_INF = -1e30
UNITS = SEQ // (2 * CHUNK)
PAD = CHUNK

PIECE = 2048
HP = PIECE // 2
STAGES = 4
IN_PIECES = IN_W // 256
OUT_PIECES = 4
FF_BLOCK = 256
FF_BLOCKS = FF // FF_BLOCK
GATE_PIECES = D // 256
FF_FIRST = IN_PIECES + OUT_PIECES
GATE_FIRST = FF_FIRST + 2 * FF_BLOCKS

IN_GROUPS = 4 * IN_PIECES
L_GROUPS = 16
A_GROUPS = 16
L0 = IN_GROUPS
A0 = L0 + L_GROUPS
MAIN_GROUPS = A0 + A_GROUPS
MAIN = 3
GATE_AT = [4, 8, 12, 16]

H_MIX, H_LRU, H_ATT, H_FFN, H_PLE = 0, 16, 24, 32, 48
SS_MIX, SS_LRU, SS_ATT, SS_FFN, SS_PLE, SS_FIN = 0, 2, 4, 6, 8, 10
SQ_TILES = [8, 8, 4, 4, 4, 4, 8, 8, 8, 8, 8, 8]
SQ_BY = [sum(SQ_TILES[:n + 1]) for n in range(len(SQ_TILES))]
RING = 2
RING_FREE = 2


def build(nc, x, p, g_mix, w_in, w_conv, b_conv, w_lru_a, b_lru_a, w_lru_i, b_lru_i, lru_lambda,
          sinks, g_lru_out, g_attn_out, w_out, g_ffn, w_ff1, w_ff2, g_ple, w_ple_gate, w_ple_proj,
          g_final, alibi, out):
    ctx = ExitStack()
    with ctx:
        KB = 1024
        base = -(-(nc.sbuf_base) // 32) * 32

        def at(name, offset, shape, dt=F32):
            return nc.alloc_sbuf_tensor_at(name, shape, dt, offset=base + offset)

        def sem(name):
            return ctx.enter_context(nc.semaphore(name))

        XT, HH, HL, WH, WL, ST = 0, 32 * KB, 64 * KB, 96 * KB, 112 * KB, 128 * KB
        T, Y, G, Q = 144 * KB, 160 * KB, 176 * KB, 192 * KB
        KV = 208 * KB
        xT = at("xT", XT, [P, KD, SEQ])
        h_hi = at("h_hi", HH, [P, KD, SEQ], F32R)
        h_lo = at("h_lo", HL, [P, KD, SEQ], F32R)
        w_hi = at("w_hi", WH, [P, 2, PIECE], F32R)
        w_lo = at("w_lo", WL, [P, 2, PIECE], F32R)
        stage = at("stage", ST, [P, STAGES, HP])
        x_nat = at("x_nat", Y, [P, TT, D])
        gate_w = at("gate_w", Q, [P, 2, LT, P])
        rows = at("rows", Q + 4 * KB, [64, P])
        sq = at("sq", T, [P, RING, HALF])
        acc = at("acc", T + 4 * KB, [P, SEQ])
        lru_r = at("lru_r", T, [P, SEQ])
        lru_i = at("lru_i", T + 4 * KB, [P, SEQ])
        lru_u = at("lru_u", T + 8 * KB, [P, SEQ])
        lru_x = at("lru_x", T + 12 * KB, [P, SEQ])
        yl = at("yl", Y, [P, LT, SEQ])
        gl = at("gl", G, [P, LT, SEQ])
        r_lru = at("r_lru", G + 4 * KB, [P, SEQ])
        qT = at("qT", Q, [P, SEQ // CHUNK, LT, CHUNK])
        kT = at("kT", KV, [P, PAD + SEQ])
        vT = at("vT", KV + 4 * (PAD + SEQ), [P, PAD + SEQ])
        v_win = at("v_win", T + 8 * KB, [P, SEQ // CHUNK, P])
        prob = at("prob", G, [P, 2, 1024])
        probT = at("probT", G + 8 * KB, [P, 1024])
        bias = at("bias", G + 12 * KB, [P, 512])
        scaled = at("scaled", T + 8 * KB, [P, 2, HALF])
        r_ffn = at("r_ffn", T + 12 * KB, [P, SEQ])
        vn = at("vn", Q, [P, 4, HALF])
        u_hi = at("u_hi", Y, [P, 2, SEQ], F32R)
        u_lo = at("u_lo", Y + 8 * KB, [P, 2, SEQ], F32R)
        relu = at("relu", G, [P, 2, HALF])
        usq = at("usq", G + 4 * KB, [P, 2, HALF])
        p_nat = at("p_nat", G + 8 * KB, [P, TT, PLE])
        pT_hi = at("pT_hi", T, [P, 2, SEQ], F32R)
        pT_lo = at("pT_lo", T + 8 * KB, [P, 2, SEQ], F32R)
        pw_hi = at("pw_hi", Q, [P, PIECE], F32R)
        pw_lo = at("pw_lo", Q + 8 * KB, [P, PIECE], F32R)
        gt = at("gt", G, [P, 2, HALF])
        sq2 = at("sq2", Y, [P, RING, HALF])
        acc2 = at("acc2", Y + 4 * KB, [P, SEQ])
        o_nat = at("o_nat", Y + 8 * KB, [P, 2, D])
        g_fin = at("g_fin", KV, [P, D])
        at_byte = KV + 2 * 4 * (PAD + SEQ)
        small = {}
        for name, shape in (("r_mix", [P, SEQ]), ("ident", [P, P]), ("ones", [P, P]), ("vec", [P, 64]),
                            ("snk", [P, NQ]), ("sink", [P, 8]), ("nsink", [P, 8]), ("eps", [P, 1]),
                            ("lam", [P, 6, LT]), ("nmax", [P, 2, 8]), ("smax", [P, 2, 8]),
                            ("esink", [P, 2, 8]), ("den", [P, 2, 8]), ("rnat", [P, 8])):
            small[name] = at(name, at_byte, shape)
            at_byte += -(-4 * int(np.prod(shape[1:])) // 32) * 32
        r_mix, ident, ones, vec = (small[n] for n in ("r_mix", "ident", "ones", "vec"))
        snk, sink, nsink, eps, lam = (small[n] for n in ("snk", "sink", "nsink", "eps", "lam"))
        nmax, smax, esink, den, rnat = (small[n] for n in ("nmax", "smax", "esink", "den", "rnat"))
        v_mix, v_conv, v_bconv = vec[:, 0:8], vec[:, 8:24], vec[:, 24:28]
        v_ba, v_bi, v_lam = vec[:, 28:32], vec[:, 32:36], vec[:, 36:40]
        v_lru, v_att, v_ffn, v_ple = vec[:, 40:44], vec[:, 44:48], vec[:, 48:56], vec[:, 56:64]
        c_tanh, c_exp = lam[:, 4, :], lam[:, 5, :]

        bank = [ctx.enter_context(nc.psum_tensor(f"bank{i}", [P, HALF], F32)) for i in range(8)]

        x_in = [sem(f"x_in{t}") for t in range(TT)]
        stage_in = [sem(f"stage_in{i}") for i in range(STAGES)]
        vec_in, gatew_in, bias_in, sink_in = sem("vec_in"), sem("gatew_in"), sem("bias_in"), sem("sink_in")
        p_in, gfin_in, out_done = sem("p_in"), sem("gfin_in"), [sem("out_done0"), sem("out_done1")]
        consts, gatew_zero, w_split, sq_used, p_ready, pool_chain = (
            sem(n) for n in ("consts", "gatew_zero", "w_split", "sq_used", "p_ready", "pool_chain"))
        xt_done, vec_t, main_done, gates_done, ss_done, vt_done, s_done, pt_done, o_done = (
            sem(n) for n in ("xt_done", "vec_t", "main_done", "gates_done", "ss_done", "vt_done", "s_done",
                             "pt_done", "o_done"))
        ff1_done, ff2_done, pp_done, gate_done, ple_done, nat_done, ssn_done = (
            sem(n) for n in ("ff1_done", "ff2_done", "pp_done", "gate_done", "ple_done", "nat_done", "ssn_done"))
        w_high, h_high, sq_done, rms_done, lam_exp, gates_sig, lru_tanh, lru_exp, lru_root = (
            sem(n) for n in ("w_high", "h_high", "sq_done", "rms_done", "lam_exp", "gates_sig", "lru_tanh",
                             "lru_exp", "lru_root"))
        gelu_done, vt_read, exp_done, pt0_read, relu_done, u_high, pp_high, gate_sig, rnat_root = (
            sem(n) for n in ("gelu_done", "vt_read", "exp_done", "pt0_read", "relu_done", "u_high", "pp_high",
                             "gate_sig", "rnat_root"))
        dve_chain, vec_ready, lam_abs, lam_ready, x_copied, h_ready, main_free, conv_done, lru_m2, state_done = (
            sem(n) for n in ("dve_chain", "vec_ready", "lam_abs", "lam_ready", "x_copied", "h_ready",
                             "main_free", "conv_done", "lru_m2", "state_done"))
        y_done, y_normed, s_read, max_done, den_done, pt1_read, o_read, sink_ready, pads_ready = (
            sem(n) for n in ("y_done", "y_normed", "s_read", "max_done", "den_done", "pt1_read", "o_read",
                             "sink_ready", "pads_ready"))
        vn_done, u_sq, u_ready, y_added, pp_ready, gate_scaled, x_gated, rnat_ready, nat_read = (
            sem(n) for n in ("vn_done", "u_sq", "u_ready", "y_added", "pp_ready", "gate_scaled", "x_gated",
                             "rnat_ready", "nat_read"))

        def half(hf):
            return slice(hf * HALF, (hf + 1) * HALF)

        def by_heads(n, raw, split):
            if n not in (5, 6):
                return raw, split
            return (raw.rearrange("p (k g j d) -> p j k g d", k=KD // 2, g=NKV, d=HD),
                    split.rearrange("p (k j g d) -> p j k g d", k=KD // 2, g=NKV, d=HD))

        def q_tile(j, hf):
            return qT[:, hf * 8:(hf + 1) * 8, j, :]

        def by_chunk(ap):
            return ap.rearrange("p (c q) -> p c q", q=CHUNK)

        def slot(n):
            return (n - (n > GATE_FIRST)) % 2

        def piece_free(eng, n):
            if n < IN_PIECES:
                eng.wait_ge(main_done, 4 * (n + 1))
            else:
                eng.wait_ge(main_done, IN_GROUPS + 8 * (n - IN_PIECES + 1))

        block = ctx.enter_context(nc.Block())

        @block.sync
        def _(sp):
            def load_x(t):
                sp.dma_start(x_nat[:, t, :], x[t * P:(t + 1) * P, :]).then_inc(x_in[t], 16)

            def load_piece(n, w, k0, kt, c0, cols):
                src = w.rearrange("(k p) c -> p k c", p=P)
                for s in (2 * n, 2 * n + 1):
                    if s >= STAGES:
                        sp.wait_ge(w_split, s - STAGES + 1)
                    kk = k0 + (s % 2) * (kt // 2)
                    dst = stage[:, s % STAGES, :].rearrange("p (k c) -> p k c", k=kt // 2)
                    sp.dma_start(dst, src[:, kk:kk + kt // 2, c0:c0 + cols]).then_inc(stage_in[s % STAGES], 16)

            for t in range(4):
                load_x(t)
            for n in range(IN_PIECES):
                if n == 1:
                    for t in range(4, TT):
                        load_x(t)
                if n < 4:
                    load_piece(n, w_in, 0, KD, n * 256, 256)
                elif n == 4:
                    load_piece(n, w_in, 0, KD, 2 * LRU + ATT, 256)
                else:
                    i = n - 5
                    src = w_in.rearrange("(k p) c -> p k c", p=P)
                    for s in (2 * n, 2 * n + 1):
                        sp.wait_ge(w_split, s - STAGES + 1)
                        kk = (s % 2) * 4
                        dst = stage[:, s % STAGES, :].rearrange("p (k c) -> p k c", k=4)
                        for g in range(NKV):
                            c0 = 2 * LRU + g * 256 + i * 128
                            sp.dma_start(dst[:, :, g * 128:(g + 1) * 128],
                                         src[:, kk:kk + 4, c0:c0 + 128]).then_inc(stage_in[s % STAGES], 16)
            for i in range(2):
                load_piece(IN_PIECES + i, w_out, 0, LT, i * 512, 512)
            sp.wait_ge(y_done, LT)
            sp.dma_start(bias[:, :], alibi).then_inc(bias_in, 16)
            att_rows = w_out[LRU:, :].rearrange("(g j d) c -> g d j c", g=NKV, d=HD)
            for i in range(2):
                n = IN_PIECES + 2 + i
                for s in (2 * n, 2 * n + 1):
                    sp.wait_ge(w_split, s - STAGES + 1)
                    j0 = (s % 2) * 2
                    dst = stage[:, s % STAGES, :].rearrange("p (k c) -> p k c", k=2)
                    for g in range(NKV):
                        sp.dma_start(dst[g * HD:(g + 1) * HD, :, :],
                                     att_rows[g, :, j0:j0 + 2, i * 512:(i + 1) * 512]
                                     ).then_inc(stage_in[s % STAGES], 16)
            w1 = w_ff1.rearrange("(k p) c -> p k c", p=P)
            w2 = w_ff2.rearrange("(b h p) c -> b h p c", h=2, p=P)
            with sp.Fori(0, FF_BLOCKS) as b:
                for i in range(4):
                    s0 = 2 * FF_FIRST + i
                    sp.wait_ge(w_split, 4 * b + (s0 - STAGES + 1))
                    if i < 2:
                        sp.dma_start(stage[:, s0 % STAGES, :].rearrange("p (k c) -> p k c", k=4),
                                     w1[:, 4 * i:4 * i + 4, bass.ds(b * FF_BLOCK, FF_BLOCK)]
                                     ).then_inc(stage_in[s0 % STAGES], 16)
                    else:
                        sp.dma_start(stage[:, s0 % STAGES, :], w2[b, i - 2]).then_inc(stage_in[s0 % STAGES], 16)
            sp.wait_ge(main_done, MAIN_GROUPS)
            sp.dma_start(p_nat[:, :, :], p.rearrange("(t q) c -> q t c", q=P)).then_inc(p_in, 16)
            sp.dma_start(g_fin[:, :], g_final.rearrange("(a d) -> a d", a=1).to_broadcast([P, D])).then_inc(gfin_in, 16)
            for i in range(9):
                n = GATE_FIRST + i
                if i == 1:
                    load_piece(n, w_ple_proj, 0, 2, 0, D)
                else:
                    c = (0 if i == 0 else i - 1) % GATE_PIECES
                    load_piece(n, w_ple_gate, 0, KD, c * 256, 256)
            for t in range(TT):
                sp.wait_ge(nat_read, 2 * (t + 1))
                sp.dma_start(out[t * P:(t + 1) * P, :], o_nat[:, t % 2, :]).then_inc(out_done[t % 2], 16)
            for i in range(2):
                sp.wait_ge(out_done[i], 16 * TT // 2)

        @block.gpsimd
        def _(pool):
            pool.memset(ident[:, :], 0.0).then_inc(pool_chain, 1)
            pool.memset(ones[:, :], 1.0).then_inc(consts, 1)
            pool.memset(eps[:, :], EPS).then_inc(consts, 1)
            pool.memset(gate_w[:, :, :, :], 0.0).then_inc(gatew_zero, 1)
            pool.wait_ge(pool_chain, 1)
            pool.affine_select(out=ident[:, :], in_=ident[:, :], compare_op=ALU.not_equal, fill=1.0,
                               base=0, pattern=[[-1, P]], channel_multiplier=1).then_inc(consts, 1)

            def low(s, dst=None):
                n = s // 2
                pool.wait_ge(w_high, s + 1)
                o = (s % 2) * HP
                lo, hi = (w_lo[:, slot(n), o:o + HP], w_hi[:, slot(n), o:o + HP]) if dst is None else dst
                raw, low_part = by_heads(n, stage[:, s % STAGES, :], lo)
                pool.tensor_tensor(low_part, raw, by_heads(n, stage[:, s % STAGES, :], hi)[1], ALU.subtract).then_inc(w_split, 1)

            def add_square(n, i, ring, total):
                q = SQ_BY[n] - SQ_TILES[n] + i
                if n >= 2 and i == 0:
                    pool.wait_ge(ss_done, n - 1)
                pool.wait_ge(sq_done, q + 1)
                dst, src = total[:, half(n % 2)], ring[:, q % RING, :]
                if i == 0:
                    pool.tensor_copy(dst, src).then_inc(sq_used, 1)
                else:
                    pool.wait_ge(sq_used, q)
                    pool.tensor_tensor(dst, dst, src, ALU.add).then_inc(sq_used, 1)

            def sums(n, ring, total):
                for i in range(SQ_TILES[n]):
                    add_square(n, i, ring, total)

            def probs(u):
                pool.wait_ge(den_done, u + 1)
                e = prob[:, u % 2, :].rearrange("p (b k) -> p b k", k=P)
                pool.tensor_tensor(e, e, den[:, u % 2, :].unsqueeze(2).to_broadcast([P, 8, P]),
                                   ALU.mult).then_inc(p_ready, 1)

            low(0)
            low(1)
            sums(SS_MIX, sq, acc)
            low(2)
            low(3)
            sums(SS_MIX + 1, sq, acc)
            for n in range(2, IN_PIECES):
                low(2 * n)
                low(2 * n + 1)
                if n == 6:
                    sums(SS_LRU, sq, acc)
                    sums(SS_LRU + 1, sq, acc)
            low(2 * 7)
            low(2 * 7 + 1)
            probs(0)
            low(2 * 8)
            low(2 * 8 + 1)
            probs(1)
            for p_ in range(8):
                if p_ == 4:
                    low(2 * 9)
                    low(2 * 9 + 1)
                if p_ + 2 < UNITS:
                    probs(p_ + 2)
            sums(SS_ATT, sq, acc)
            low(2 * 10)
            low(2 * 10 + 1)
            sums(SS_ATT + 1, sq, acc)
            sums(SS_FFN, sq, acc)
            low(2 * FF_FIRST)
            low(2 * FF_FIRST + 1)
            sums(SS_FFN + 1, sq, acc)
            with pool.Fori(0, FF_BLOCKS) as b:
                for i in range(4):
                    s0 = 2 * FF_FIRST + 2 + i
                    n0, o = s0 // 2, (s0 % 2) * HP
                    pool.wait_ge(w_high, 4 * b + (s0 + 1))
                    pool.tensor_tensor(w_lo[:, n0 % 2, o:o + HP], stage[:, s0 % STAGES, :],
                                       w_hi[:, n0 % 2, o:o + HP], ALU.subtract).then_inc(w_split, 1)
            sums(SS_PLE, sq2, acc2)
            s0 = 2 * (GATE_FIRST + 1)
            for s in (s0, s0 + 1):
                o = (s % 2) * HP
                low(s, (pw_lo[:, o:o + HP], pw_hi[:, o:o + HP]))
            low(s0 + 2)
            low(s0 + 3)
            sums(SS_PLE + 1, sq2, acc2)
            for q in range(2 * KD):
                if q >= 2:
                    add_square(SS_FIN + (q - 2) // KD, (q - 2) % KD, sq2, acc2)
                if q % 2 == 1 and q // 2 < 6:
                    low(2 * (GATE_FIRST + 3 + q // 2))
                    low(2 * (GATE_FIRST + 3 + q // 2) + 1)
            for q in (KD - 2, KD - 1):
                add_square(SS_FIN + 1, q, sq2, acc2)

        @block.tensor
        def _(pe):
            def passes(o, whi, wlo, hh, hl, first, last):
                pe.matmul(o, whi, hh, start=first, stop=False)
                pe.matmul(o, whi, hl, start=False, stop=False)
                return pe.matmul(o, wlo, hh, start=False, stop=last)

            def group(g, n, kt, m, hf, k_h, h_first, ready):
                cols = PIECE // kt
                if g >= MAIN:
                    pe.wait_ge(main_free, g - MAIN + 1)
                o = bank[g % MAIN][:, :]
                for k in range(kt):
                    if ready and k == 0:
                        pe.wait_ge(w_split, 2 * n + 1)
                    if ready and k == kt // 2:
                        pe.wait_ge(w_split, 2 * n + 2)
                    if h_first is not None:
                        pe.wait_ge(h_ready, h_first + k + 1)
                    c = k * cols + m * P
                    sl = [w[:, n % 2, c:c + P] for w in (w_hi, w_lo)]
                    hh, hl = h_hi[:, k_h + k, half(hf)], h_lo[:, k_h + k, half(hf)]
                    last = passes(o, sl[0], sl[1], hh, hl, k == 0, k == kt - 1)
                last.then_inc(main_done, 1)

            def turn_x(hf):
                for k in range(KD):
                    e = KD * hf + k
                    if e >= 4:
                        pe.wait_ge(x_copied, e - 3)
                    for t in range(4):
                        if k == 0:
                            pe.wait_ge(x_in[4 * hf + t], 16)
                        last = pe.transpose(bank[4 + e % 4][:, t * P:(t + 1) * P],
                                            x_nat[:, 4 * hf + t, k * P:(k + 1) * P], ident[:, :])
                    last.then_inc(xt_done, 1)

            def sum_rows(n, total, b):
                pe.wait_ge(sq_used, SQ_BY[n])
                if n >= 1:
                    pe.wait_ge(rms_done, n)
                pe.matmul(bank[b][:, :], ones[:, :], total[:, half(n % 2)], start=True, stop=True
                          ).then_inc(ss_done, 1)

            def gates(j):
                pe.wait_ge(gatew_in, 64)
                pe.wait_ge(conv_done, j + 1)
                for hf in range(2):
                    for i in range(2):
                        b = 4 + 2 * hf + i
                        if j >= 1:
                            pe.wait_ge(gates_sig, 4 * (j - 1) + 2 * hf + i + 1)
                        else:
                            pe.wait_ge(x_copied, 2 * KD)
                        pe.matmul(bank[b][:, :], gate_w[:, i, j, :], lru_x[:, half(hf)], start=True, stop=True
                                  ).then_inc(gates_done, 1)

            def turn_v(i):
                pe.wait_ge(main_free, 4 * 4 + 4)
                pe.wait_ge(pads_ready, 2)
                if i >= 2:
                    pe.wait_ge(vt_read, i - 1)
                else:
                    pe.wait_ge(gates_sig, 16)
                for c in range(4 * i, 4 * i + 4):
                    last = pe.transpose(bank[6 + i % 2][:, (c % 4) * P:(c % 4 + 1) * P],
                                        vT[:, c * CHUNK:c * CHUNK + P], ident[:, :])
                last.then_inc(vt_done, 1)

            def scores(u):
                pe.wait_ge(main_free, IN_GROUPS - 2 + (2 if u >= UNITS // 2 else 0))
                for g in range(NKV):
                    if u >= 1:
                        pe.wait_ge(s_read, 2 * (u - 1) + g + 1)
                    r = slice(g * HD, (g + 1) * HD)
                    for cp in range(2):
                        c = 2 * u + cp
                        for a in range(2):
                            last = pe.matmul(bank[4 + g][:, (2 * cp + a) * P:(2 * cp + a + 1) * P],
                                             qT[r, c, 2 * a:2 * a + 2, :].rearrange("p a q -> p (a q)"),
                                             kT[r, c * CHUNK:c * CHUNK + P], start=True, stop=True)
                    last.then_inc(s_done, 1)

            def turn_p(u):
                pe.wait_ge(p_ready, u + 1)
                for g in range(NKV):
                    if u >= 1:
                        pe.wait_ge(pt0_read if g == 0 else pt1_read, u)
                    else:
                        pe.wait_ge(vt_read, 4)
                    for i in range(4):
                        last = pe.transpose(bank[6 + g][:, i * P:(i + 1) * P],
                                            prob[:, u % 2, (4 * g + i) * P:(4 * g + i + 1) * P], ident[:, :])
                    last.then_inc(pt_done, 1)

            def values(u):
                pe.wait_ge(pt0_read, u + 1)
                pe.wait_ge(pt1_read, u + 1)
                if u >= 1:
                    pe.wait_ge(o_read, u)
                for cp in range(2):
                    for g in range(NKV):
                        last = pe.matmul(bank[3][g * HD:(g + 1) * HD, cp * 256:(cp + 1) * 256],
                                         v_win[:, 2 * u + cp, g * HD:(g + 1) * HD],
                                         probT[:, g * 512 + cp * 256:g * 512 + (cp + 1) * 256],
                                         start=True, stop=True)
                last.then_inc(o_done, 1)

            pe.wait_ge(consts, 3)
            pe.wait_ge(vec_in, 16 * 12)
            pe.transpose(bank[3][:, 0:64], rows[:, :], ident[0:64, 0:64]).then_inc(vec_t, 1)
            turn_x(0)
            for g in range(IN_GROUPS):
                n, hf, m = g // 4, (g % 4) // 2, g % 2
                if g == 2:
                    turn_x(1)
                group(g, n, KD, m, hf, 0, H_MIX + 8 * hf if g in (0, 2) else None, g % 4 == 0)
                if g == 1:
                    pe.wait_ge(vec_ready, 1)
                    sum_rows(SS_MIX, acc, 3)
                if g == 2:
                    sum_rows(SS_MIX + 1, acc, 3)
                if g in GATE_AT:
                    gates(GATE_AT.index(g))
                if 20 <= g < 24:
                    turn_v(g - 20)
                if g == 24:
                    sum_rows(SS_LRU, acc, 3)
                if g == 25:
                    sum_rows(SS_LRU + 1, acc, 3)
                if g == 26:
                    scores(0)
            scores(1)
            pe.wait_ge(rms_done, SS_LRU + 2)
            for u in range(UNITS):
                for i in range(2):
                    g = 2 * u + i
                    n, hf, m = g // 8, (g % 8) // 4, g % 4
                    group(L0 + g, IN_PIECES + n, LT, m, hf, 0, H_LRU + 4 * hf if n == 0 and m == 0 else None,
                          g % 8 == 0)
                    if i == 0:
                        turn_p(u)
                        if u + 2 < UNITS:
                            scores(u + 2)
                values(u)
            for g in range(A_GROUPS):
                n, hf, m = g // 8, (g % 8) // 4, g % 4
                group(A0 + g, IN_PIECES + 2 + n, LT, m, hf, LT, H_ATT + 4 * hf if n == 0 and m == 0 else None,
                      g % 8 == 0)
                if g == 0:
                    pe.wait_ge(o_read, UNITS)
                    sum_rows(SS_ATT, acc, 3)
                if g == 2:
                    sum_rows(SS_ATT + 1, acc, 3)
                if g == 13:
                    sum_rows(SS_FFN, acc, 7)
            sum_rows(SS_FFN + 1, acc, 7)

            pe.wait_ge(main_free, MAIN_GROUPS)
            pe.wait_ge(rms_done, SS_FFN)
            pe.wait_ge(s_read, 2 * UNITS)
            pe.sem_inc(relu_done, 4)
            pe.sem_inc(y_added, 4)
            n1, n2 = FF_FIRST % 2, (FF_FIRST + 1) % 2
            with pe.Fori(0, FF_BLOCKS) as b:
                pe.wait_ge(w_split, 4 * b + 2 * (FF_FIRST + 1))
                for hf in range(2):
                    for m in range(2):
                        j = 2 * hf + m
                        pe.wait_ge(relu_done, 4 * b + (j + 1))
                        for k in range(KD):
                            if m == 0:
                                pe.wait_ge(h_ready, H_FFN + 8 * hf + k + 1)
                            c = k * 256 + m * P
                            hh, hl = h_hi[:, k, half(hf)], h_lo[:, k, half(hf)]
                            last = passes(bank[j][:, :], w_hi[:, n1, c:c + P], w_lo[:, n1, c:c + P], hh, hl,
                                          k == 0, k == KD - 1)
                        last.then_inc(ff1_done, 1)
                pe.wait_ge(w_split, 4 * b + 2 * (FF_FIRST + 2))
                for hf in range(2):
                    pe.wait_ge(u_ready, 4 * b + (2 * hf + 2 + RING_FREE))
                    for m in range(KD):
                        q = KD * hf + m
                        o = bank[4 + q % 4][:, :]
                        pe.wait_ge(y_added, 16 * b + (q + 1))
                        for k in range(2):
                            c = k * D + m * P
                            hh, hl = u_hi[:, k, half(hf)], u_lo[:, k, half(hf)]
                            last = passes(o, w_hi[:, n2, c:c + P], w_lo[:, n2, c:c + P], hh, hl, k == 0, k == 1)
                        last.then_inc(ff2_done, 1)

            pe.wait_ge(p_in, 16)
            pe.wait_ge(y_added, 4 + 16 * FF_BLOCKS)
            pe.wait_ge(relu_done, 4 + 4 * FF_BLOCKS)
            for i in range(4):
                k, hf = i % 2, i // 2
                for t in range(4):
                    last = pe.transpose(bank[4 + i][:, t * P:(t + 1) * P],
                                        p_nat[:, 4 * hf + t, k * P:(k + 1) * P], ident[:, :])
                last.then_inc(pp_done, 1)

            def gate(hf, i, m):
                n = GATE_FIRST + (0 if hf == 0 and i == 0 else 1 + i + 4 * hf)
                q = KD * hf + 2 * i + m
                if q >= 2:
                    pe.wait_ge(gate_scaled, q - 1)
                if m == 0:
                    pe.wait_ge(w_split, 2 * n + 2)
                for k in range(KD):
                    if i == 0 and m == 0:
                        pe.wait_ge(h_ready, H_PLE + 8 * hf + k + 1)
                    c = k * 256 + m * P
                    hh, hl = h_hi[:, k, half(hf)], h_lo[:, k, half(hf)]
                    o = bank[q % 2][:, :]
                    last = passes(o, w_hi[:, slot(n), c:c + P], w_lo[:, slot(n), c:c + P], hh, hl, k == 0, k == KD - 1)
                last.then_inc(gate_done, 1)

            def project(hf, m):
                q = KD * hf + m
                if q == 0:
                    pe.wait_ge(w_split, 2 * (GATE_FIRST + 1) + 2)
                if m == 0:
                    pe.wait_ge(pp_ready, 2 * hf + 2)
                if q >= 2:
                    pe.wait_ge(x_gated, 2 * (q - 2) + 1)
                for k in range(2):
                    c = k * D + m * P
                    hh, hl = pT_hi[:, k, half(hf)], pT_lo[:, k, half(hf)]
                    o = bank[2 + q % 2][:, :]
                    last = passes(o, pw_hi[:, c:c + P], pw_lo[:, c:c + P], hh, hl, k == 0, k == 1)
                last.then_inc(ple_done, 1)

            def sum_nat(hf):
                pe.wait_ge(sq_used, SQ_BY[SS_FIN + hf])
                if hf == 0:
                    pe.wait_ge(rms_done, SS_PLE + 2)
                else:
                    pe.wait_ge(gate_scaled, 2 * KD)
                for t in range(4):
                    last = pe.matmul(bank[4 - 4 * hf][:, t:t + 1],
                                     acc2[:, hf * HALF + t * P:hf * HALF + (t + 1) * P],
                                     ones[:, 0:1], start=True, stop=True)
                last.then_inc(ssn_done, 1)

            def turn_out(t):
                if t < 4:
                    pe.wait_ge(rnat_root, 1)
                pe.wait_ge(x_gated, 2 * (KD * (t // 4) + KD))
                if t >= 2:
                    pe.wait_ge(nat_read, 2 * (t - 1))
                for b in range(2):
                    for k in range(4):
                        last = pe.transpose(bank[(6 if t % 2 == 0 else 4) + b][:, k * P:(k + 1) * P],
                                            xT[:, 4 * b + k, t * P:(t + 1) * P], ident[:, :])
                    last.then_inc(nat_done, 1)

            for hf in range(2):
                for i in range(GATE_PIECES):
                    for m in range(2):
                        gate(hf, i, m)
                    for m in range(2):
                        project(hf, 2 * i + m)
                    if hf == 0 and i == 0:
                        pe.wait_ge(pp_ready, 4)
                        sum_rows(SS_PLE, acc2, 4)
                    if hf == 0 and i == 1:
                        sum_rows(SS_PLE + 1, acc2, 4)
                    if hf == 1 and i == 1:
                        sum_nat(0)
                    if hf == 1 and i >= 2:
                        turn_out(2 * i - 4)
                        turn_out(2 * i - 3)
            turn_out(4)
            turn_out(5)
            sum_nat(1)
            turn_out(6)
            turn_out(7)

        @block.scalar
        def _(act):
            def row(i, v, n):
                act.dma_start(rows[i:i + n, :], v.rearrange("(k q) -> k q", q=P)).then_inc(vec_in, 16)

            row(0, g_mix, 8)
            act.dma_start(rows[8:24, :], w_conv.rearrange("c (k q) -> (c k) q", q=P)).then_inc(vec_in, 16)
            row(24, b_conv, 4)
            row(28, b_lru_a, 4)
            row(32, b_lru_i, 4)
            row(36, lru_lambda, 4)
            row(40, g_lru_out, 4)
            for g in range(NKV):
                act.dma_start(rows[44:48, g * HD:(g + 1) * HD],
                              g_attn_out[g * 256:(g + 1) * 256].rearrange("(j d) -> j d", d=HD)
                              ).then_inc(vec_in, 16)
            row(48, g_ffn, 8)
            row(56, g_ple, 8)
            act.dma_start(snk[:, :], sinks.rearrange("(a d) -> a d", a=1).to_broadcast([P, NQ])).then_inc(vec_in, 16)
            act.wait_ge(gatew_zero, 1)
            for i, w in enumerate((w_lru_a, w_lru_i)):
                for b in range(2):
                    act.dma_start(gate_w[b * HD:(b + 1) * HD, i, :, b * HD:(b + 1) * HD],
                                  w.rearrange("(j b) c d -> b c j d", b=2)[b]).then_inc(gatew_in, 16)

            def high(s, dst=None):
                n = s // 2
                act.wait_ge(stage_in[s % STAGES], stage_count(s))
                o = (s % 2) * HP
                hi = w_hi[:, slot(n), o:o + HP] if dst is None else dst
                raw, high_part = by_heads(n, stage[:, s % STAGES, :], hi)
                act.activation(high_part, raw, ACT.Copy).then_inc(w_high, 1)

            def stage_count(s):
                two = [14 - 4, 14 - 3, 14 - 2, 14 - 1] + [2 * (IN_PIECES + 2) + i for i in range(4)]
                return sum(32 if q in two else 16 for q in range(s % STAGES, s + 1, STAGES))

            def split_high(i, src, scale, k, hf):
                dst = h_hi[:, k, half(hf)]
                if H_ATT <= i < H_FFN:
                    dst = by_chunk(dst)
                if scale is None:
                    act.activation(dst, src, ACT.Copy).then_inc(h_high, 1)
                else:
                    act.activation(dst, src, ACT.Copy, scale=scale).then_inc(h_high, 1)

            def square(q, ring, src):
                if q >= RING:
                    act.wait_ge(sq_used, q - RING + 1)
                dst = ring[:, q % RING, :]
                if SQ_BY[SS_LRU + 1] <= q < SQ_BY[SS_ATT + 1]:
                    dst = by_chunk(dst)
                act.activation(dst, src, ACT.Square).then_inc(sq_done, 1)

            def root(n, b, dst, width):
                act.wait_ge(ss_done, n + 1)
                act.activation(dst[:, half(n % 2)], bank[b][:, :], ACT.Sqrt, bias=eps[:, 0:1],
                               scale=1.0 / width).then_inc(rms_done, 1)

            act.wait_ge(consts, 3)
            for hf in range(2):
                if hf == 0:
                    act.wait_ge(vec_ready, 1)
                for k in range(KD):
                    act.wait_ge(x_copied, KD * hf + k + 1)
                    split_high(H_MIX + KD * hf + k, xT[:, k, half(hf)], v_mix[:, k:k + 1], k, hf)
                    square(KD * hf + k, sq, xT[:, k, half(hf)])
                    if k == 1:
                        high(2 * hf)
                        high(2 * hf + 1)
                if hf == 0:
                    act.wait_ge(lam_abs, 1)
                    act.activation(lam[:, 1, :], lam[:, 0, :], ACT.Exp, scale=-1.0).then_inc(lam_exp, 1)
                root(SS_MIX + hf, 3, r_mix, D)

            def lru_gates(j):
                act.wait_ge(lam_ready, 1)
                if j >= 1:
                    act.wait_ge(state_done, j)
                for hf in range(2):
                    for i, (dst, bv) in enumerate(((lru_r, v_ba), (lru_i, v_bi))):
                        act.wait_ge(gates_done, 4 * j + 2 * hf + i + 1)
                        act.activation(dst[:, half(hf)], bank[4 + 2 * hf + i][:, :], ACT.Sigmoid,
                                       bias=bv[:, j:j + 1]).then_inc(gates_sig, 1)
                act.wait_ge(gates_sig, 4 * j + 4)
                act.activation(lru_u[:, :], lru_r[:, :], ACT.Tanh, scale=c_tanh[:, j:j + 1]).then_inc(lru_tanh, 1)
                act.wait_ge(lru_tanh, j + 1)
                act.activation(lru_r[:, :], lru_r[:, :], ACT.Exp, scale=c_exp[:, j:j + 1]).then_inc(lru_exp, 1)

            for g in range(IN_GROUPS):
                P_, r = g // 4, g % 4
                if r == 0 and P_ >= 1:
                    n = P_ + 1
                    piece_free(act, n - 2)
                    high(2 * n)
                    high(2 * n + 1)
                if g in GATE_AT:
                    lru_gates(GATE_AT.index(g))
                if g - 1 in GATE_AT:
                    j = GATE_AT.index(g - 1)
                    act.wait_ge(lru_m2, j + 1)
                    act.activation(lru_u[:, :], lru_u[:, :], ACT.Sqrt).then_inc(lru_root, 1)
                if g in (18, 19):
                    for j in (2 * (g - 18), 2 * (g - 18) + 1):
                        act.wait_ge(main_free, 16)
                        act.activation(gl[:, j, :], gl[:, j, :], ACT.Gelu_apprx_tanh).then_inc(gelu_done, 1)
                if 20 <= g < 24:
                    i = g - 20
                    act.wait_ge(vt_done, i + 1)
                    act.wait_ge(state_done, LT)
                    act.activation(v_win[:, 4 * i:4 * i + 4, :], bank[6 + i % 2][:, :].rearrange(
                        "p (c d) -> p c d", d=P), ACT.Copy).then_inc(vt_read, 1)
                if g in (22, 23):
                    hf = g - 22
                    for j in range(LT):
                        act.wait_ge(y_done, j + 1)
                        square(SQ_BY[SS_LRU + hf] - 4 + j, sq, yl[:, j, half(hf)])
                if g in (25, 26):
                    root(SS_LRU + g - 25, 3, r_lru, LRU)

            def exps(u):
                act.wait_ge(max_done, u + 1)
                for i in range(8):
                    e = prob[:, u % 2, i * P:(i + 1) * P]
                    act.activation(e, e, ACT.Exp, bias=nmax[:, u % 2, i:i + 1],
                                   accum_out=den[:, u % 2, i:i + 1]).then_inc(exp_done, 1)
                act.activation(esink[:, u % 2, :], smax[:, u % 2, :], ACT.Exp).then_inc(exp_done, 1)

            def lru_high(hf):
                act.wait_ge(main_done, IN_GROUPS - 2 + 2 * hf)
                for j in range(LT):
                    act.wait_ge(y_normed, 4 * hf + j + 1)
                    split_high(H_LRU + 4 * hf + j, yl[:, j, half(hf)], None, j, hf)

            lru_high(0)
            exps(0)
            lru_high(1)
            piece_free(act, 6)
            high(2 * 8)
            high(2 * 8 + 1)
            exps(1)
            for u in range(UNITS):
                act.wait_ge(pt_done, 2 * u + 1)
                if u >= 1:
                    act.wait_ge(o_done, u)
                act.activation(probT[:, 0:512], bank[6][:, :], ACT.Copy).then_inc(pt0_read, 1)
                if u == 4:
                    piece_free(act, 7)
                    high(2 * 9)
                    high(2 * 9 + 1)
                if u + 2 < UNITS:
                    exps(u + 2)
                if u >= 4:
                    j = u - 4
                    act.wait_ge(o_read, 4)
                    split_high(H_ATT + j, q_tile(j, 0), v_att[:, j:j + 1], LT + j, 0)
                    square(SQ_BY[SS_ATT] - 4 + j, sq, q_tile(j, 0))
            piece_free(act, 8)
            high(2 * 10)
            high(2 * 10 + 1)
            act.wait_ge(o_read, UNITS)
            for j in range(LT):
                split_high(H_ATT + 4 + j, q_tile(j, 1), v_att[:, j:j + 1], LT + j, 1)
            root(SS_ATT, 3, r_mix, ATT)
            for j in range(LT):
                square(SQ_BY[SS_ATT + 1] - 4 + j, sq, q_tile(j, 1))
            root(SS_ATT + 1, 3, r_mix, ATT)
            for k in range(KD):
                act.wait_ge(main_free, A0 + 8 * (k // 4) + k % 4 + 1)
                square(SQ_BY[SS_FFN] - 8 + k, sq, xT[:, k, half(0)])
                if k == 3:
                    piece_free(act, 9)
                    high(2 * FF_FIRST)
                    high(2 * FF_FIRST + 1)
            root(SS_FFN, 7, r_ffn, D)
            for hf in range(2):
                act.wait_ge(main_done, MAIN_GROUPS - 4 + 4 * hf)
                for k in range(KD):
                    act.wait_ge(vn_done, KD * hf + k + 1)
                    split_high(H_FFN + KD * hf + k, vn[:, k % 4, :], None, k, hf)
                    if hf == 0:
                        act.wait_ge(main_free, A0 + 8 * (k // 4) + 4 + k % 4 + 1)
                        square(SQ_BY[SS_FFN + 1] - 8 + k, sq, xT[:, k, half(1)])
                if hf == 0:
                    root(SS_FFN + 1, 7, r_ffn, D)
            act.wait_ge(main_done, MAIN_GROUPS)
            with act.Fori(0, FF_BLOCKS) as b:
                def ff_high(i):
                    s0 = 2 * FF_FIRST + 2 + i
                    n0, o = s0 // 2, (s0 % 2) * HP
                    act.wait_ge(stage_in[s0 % STAGES], 16 * b + stage_count(s0))
                    act.activation(w_hi[:, n0 % 2, o:o + HP], stage[:, s0 % STAGES, :],
                                   ACT.Copy).then_inc(w_high, 1)

                act.wait_ge(y_added, 16 * b + 4)
                ff_high(0)
                ff_high(1)
                for j in range(4):
                    hf, m = j // 2, j % 2
                    act.wait_ge(ff1_done, 4 * b + (j + 1))
                    act.wait_ge(u_sq, 4 * b + (j - 1 + RING_FREE))
                    act.activation(relu[:, j % 2, :], bank[j][:, :], ACT.Relu).then_inc(relu_done, 1)
                    act.wait_ge(relu_done, 4 * b + (4 + j + 1))
                    act.activation(u_hi[:, m, half(hf)], relu[:, j % 2, :], ACT.Square).then_inc(u_high, 1)
                ff_high(2)
                ff_high(3)

            def ple_high(hf):
                for k in range(KD):
                    if hf == 0 or k == 0:
                        act.wait_ge(y_added, 4 + 16 * (FF_BLOCKS - 1) + KD * hf + k + 1 if hf == 0
                                    else 4 + 16 * FF_BLOCKS)
                    split_high(H_PLE + KD * hf + k, xT[:, k, half(hf)], v_ple[:, k:k + 1], k, hf)

            def project_high():
                s0 = 2 * (GATE_FIRST + 1)
                for s in (s0, s0 + 1):
                    high(s, pw_hi[:, (s % 2) * HP:(s % 2 + 1) * HP])

            def gate_high(n):
                high(2 * n)
                high(2 * n + 1)

            ple_high(0)
            for i in range(4):
                k, hf = i % 2, i // 2
                act.wait_ge(pp_done, i + 1)
                act.activation(pT_hi[:, k, half(hf)], bank[4 + i][:, :], ACT.Copy).then_inc(pp_high, 1)
            act.wait_ge(ff2_done, 16 * FF_BLOCKS)
            for k in range(KD):
                square(SQ_BY[SS_PLE] - 8 + k, sq2, xT[:, k, half(0)])
            project_high()
            gate_high(GATE_FIRST + 2)
            root(SS_PLE, 4, r_mix, D)
            ple_high(1)
            for k in range(KD):
                square(SQ_BY[SS_PLE + 1] - 8 + k, sq2, xT[:, k, half(1)])

            def sigmoid(q):
                act.wait_ge(gate_scaled, q + 1)
                act.activation(gt[:, q % 2, :], gt[:, q % 2, :], ACT.Sigmoid).then_inc(gate_sig, 1)

            def final_square(q):
                hf, k = q // KD, q % KD
                act.wait_ge(x_gated, 2 * (q + 1))
                square(SQ_BY[SS_FIN + hf] - 8 + k, sq2, xT[:, k, half(hf)])

            for q in range(2 * KD):
                sigmoid(q)
                if q >= 2:
                    final_square(q - 2)
                if q % 2 == 1 and q // 2 < 6:
                    act.wait_ge(gate_done, q + 1)
                    gate_high(GATE_FIRST + 3 + q // 2)
                if q == 4:
                    root(SS_PLE + 1, 4, r_mix, D)
                if q == KD + 3:
                    act.wait_ge(ssn_done, 1)
                    act.activation(rnat[:, 0:4], bank[4][:, 0:4], ACT.Sqrt, bias=eps[:, 0:1],
                                   scale=1.0 / D).then_inc(rnat_root, 1)
            final_square(2 * KD - 2)
            final_square(2 * KD - 1)
            act.wait_ge(ssn_done, 2)
            act.activation(rnat[:, 4:8], bank[0][:, 0:4], ACT.Sqrt, bias=eps[:, 0:1],
                           scale=1.0 / D).then_inc(rnat_root, 1)

        @block.vector
        def _(dve):
            chained = [0]

            def link(ins):
                chained[0] += 1
                ins.then_inc(dve_chain, 1)
                dve.wait_ge(dve_chain, chained[0])

            def split_low(i, src, scale, k, hf):
                dve.wait_ge(h_high, i + 1)
                o, hi = h_lo[:, k, half(hf)], h_hi[:, k, half(hf)]
                if H_ATT <= i < H_FFN:
                    o, hi = by_chunk(o), by_chunk(hi)
                if scale is None:
                    dve.tensor_tensor(o, src, hi, ALU.subtract).then_inc(h_ready, 1)
                else:
                    dve.scalar_tensor_tensor(out=o, in0=src, scalar=scale, in1=hi, op0=ALU.mult,
                                             op1=ALU.subtract).then_inc(h_ready, 1)

            def invert(n, dst):
                dve.wait_ge(rms_done, n + 1)
                link(dve.reciprocal(dst[:, half(n % 2)], dst[:, half(n % 2)]))

            def copy_x(hf, k):
                e = KD * hf + k
                dve.wait_ge(xt_done, e + 1)
                dve.tensor_copy(xT[:, k, half(hf)], bank[4 + e % 4][:, :]).then_inc(x_copied, 1)

            def evac(g):
                n, hf, m = g // 4, (g % 4) // 2, g % 2
                dve.wait_ge(main_done, g + 1)
                if n < 2:
                    dst = yl[:, 2 * n + m, half(hf)]
                elif n < 4:
                    dst = gl[:, 2 * (n - 2) + m, half(hf)]
                elif n == 4:
                    dst = (kT, vT)[m][:, PAD + hf * HALF:PAD + (hf + 1) * HALF]
                else:
                    dst = q_tile(2 * (n - 5) + m, hf)
                src, r = bank[g % MAIN][:, :], r_mix[:, half(hf)]
                if n >= 5:
                    src, r = by_chunk(src), by_chunk(r)
                dve.tensor_tensor(dst, src, r, ALU.mult).then_inc(main_free, 1)

            def decay():
                dve.wait_ge(lam_exp, 1)
                e, z, z2, s = lam[:, 1, :], lam[:, 2, :], lam[:, 3, :], lam[:, 0, :]
                link(dve.tensor_scalar(z, e, 2.0, None, ALU.add))
                link(dve.reciprocal(z, z))
                link(dve.tensor_tensor(z, z, e, ALU.mult))
                link(dve.tensor_tensor(z2, z, z, ALU.mult))
                link(dve.tensor_scalar(s, z2, 1.0 / 15.0, None, ALU.mult))
                for d in (13.0, 11.0, 9.0, 7.0, 5.0, 3.0):
                    link(dve.scalar_tensor_tensor(out=s, in0=s, scalar=1.0 / d, in1=z2, op0=ALU.add, op1=ALU.mult))
                link(dve.scalar_tensor_tensor(out=s, in0=s, scalar=1.0, in1=z, op0=ALU.add, op1=ALU.mult))
                link(dve.tensor_scalar(e, v_lam, -1.0, 0.0, ALU.mult, ALU.max))
                link(dve.scalar_tensor_tensor(out=s, in0=s, scalar=2.0, in1=e, op0=ALU.mult, op1=ALU.add))
                dve.tensor_scalar(c_tanh, s, 4.0, None, ALU.mult).then_inc(dve_chain, 1)
                chained[0] += 1
                dve.wait_ge(dve_chain, chained[0])
                dve.tensor_scalar(c_exp, s, -8.0, None, ALU.mult).then_inc(lam_ready, 1)

            def conv(j):
                if j >= 1:
                    dve.wait_ge(state_done, j)
                link(dve.tensor_scalar(lru_x[:, :], yl[:, j, :], v_conv[:, 12 + j:13 + j], v_bconv[:, j:j + 1],
                                       ALU.mult, ALU.add))
                for s in (1, 2, 3):
                    c = 4 * (3 - s) + j
                    ins = dve.scalar_tensor_tensor(out=lru_x[:, s:], in0=yl[:, j, 0:SEQ - s],
                                                   scalar=v_conv[:, c:c + 1], in1=lru_x[:, s:],
                                                   op0=ALU.mult, op1=ALU.add)
                    if s < 3:
                        link(ins)
                    else:
                        ins.then_inc(conv_done, 1)

            def decays(j):
                dve.wait_ge(lru_exp, j + 1)
                link(dve.scalar_tensor_tensor(out=lru_u[:, :], in0=lru_r[:, :], scalar=1.0, in1=lru_u[:, :],
                                              op0=ALU.add, op1=ALU.mult))
                link(dve.tensor_scalar(lru_r[:, :], lru_u[:, :], -1.0, 1.0, ALU.mult, ALU.add))
                link(dve.scalar_tensor_tensor(out=lru_u[:, :], in0=lru_r[:, :], scalar=1.0, in1=lru_u[:, :],
                                              op0=ALU.add, op1=ALU.mult))
                dve.tensor_scalar(lru_u[:, :], lru_u[:, :], 1e-34, None, ALU.max).then_inc(lru_m2, 1)
                dve.wait_ge(conv_done, j + 1)
                link(dve.tensor_tensor(lru_x[:, :], lru_i[:, :], lru_x[:, :], ALU.mult))

            def states(j):
                dve.wait_ge(lru_root, j + 1)
                link(dve.tensor_tensor(lru_x[:, :], lru_x[:, :], lru_u[:, :], ALU.mult))
                dve.tensor_tensor_scan(yl[:, j, :], lru_r[:, :], lru_x[:, :], 0.0, ALU.mult, ALU.add
                                       ).then_inc(state_done, 1)

            dve.memset(kT[:, 0:PAD], 0.0).then_inc(pads_ready, 1)
            dve.memset(vT[:, 0:PAD], 0.0).then_inc(pads_ready, 1)
            dve.wait_ge(vec_t, 1)
            dve.tensor_copy(vec[:, :], bank[3][:, 0:64]).then_inc(vec_ready, 1)
            for k in range(KD):
                copy_x(0, k)
            dve.wait_ge(vec_ready, 1)
            dve.scalar_tensor_tensor(out=lam[:, 0, :], in0=v_lam, scalar=-1.0, in1=v_lam, op0=ALU.mult,
                                     op1=ALU.max).then_inc(lam_abs, 1)
            for k in range(KD):
                split_low(H_MIX + k, xT[:, k, half(0)], v_mix[:, k:k + 1], k, 0)
            for hh in range(2):
                for cp in range(2):
                    src = snk[hh * HD:(hh + 1) * HD, :].rearrange("p (g a h) -> p g a h", g=2, a=2)[:, :, :, hh]
                    dst = sink[hh * HD:(hh + 1) * HD, :].rearrange("p (g c a) -> p g c a", g=2, c=2)[:, :, cp, :]
                    link(dve.tensor_copy(dst, src))
            link(dve.tensor_scalar(nsink[:, :], sink[:, :], -1.0, None, ALU.mult))
            for k in range(KD):
                copy_x(1, k)
            for k in range(KD):
                split_low(H_MIX + KD + k, xT[:, k, half(1)], v_mix[:, k:k + 1], k, 1)
            decay()
            invert(SS_MIX, r_mix)
            evac(0)
            evac(1)
            invert(SS_MIX + 1, r_mix)
            for g in range(2, IN_GROUPS - 2):
                evac(g)
                if g + 1 in GATE_AT:
                    dve.wait_ge(main_free, g + 1)
                    conv(GATE_AT.index(g + 1))
                if g - 1 in GATE_AT:
                    decays(GATE_AT.index(g - 1))
                if g - 2 in GATE_AT:
                    states(GATE_AT.index(g - 2))
                if g in (20, 21):
                    for j in (2 * (g - 20), 2 * (g - 20) + 1):
                        dve.wait_ge(gelu_done, j + 1)
                        dve.wait_ge(state_done, j + 1)
                        dve.tensor_tensor(yl[:, j, :], yl[:, j, :], gl[:, j, :], ALU.mult).then_inc(y_done, 1)

            def norm_y(hf):
                invert(SS_LRU + hf, r_lru)
                for j in range(LT):
                    dve.wait_ge(sq_done, SQ_BY[SS_LRU + hf] - 3 + j)
                    dve.scalar_tensor_tensor(out=yl[:, j, half(hf)], in0=yl[:, j, half(hf)],
                                             scalar=v_lru[:, j:j + 1], in1=r_lru[:, half(hf)],
                                             op0=ALU.mult, op1=ALU.mult).then_inc(y_normed, 1)

            def low_y(hf):
                for j in range(LT):
                    dve.wait_ge(y_normed, 4 * hf + j + 1)
                    split_low(H_LRU + 4 * hf + j, yl[:, j, half(hf)], None, j, hf)

            def softmax_front(u):
                if u >= 2:
                    dve.wait_ge(pt_done, 2 * (u - 1))
                s = prob[:, u % 2, :]
                for g in range(NKV):
                    dve.wait_ge(s_done, 2 * u + g + 1)
                    dve.scalar_tensor_tensor(
                        out=s[:, g * 512:(g + 1) * 512].rearrange("p (c k) -> p c k", c=2),
                        in0=bank[4 + g][:, :].rearrange("p (c k) -> p c k", c=2), scalar=HD ** -0.5,
                        in1=bias[:, g * 256:(g + 1) * 256].unsqueeze(1).to_broadcast([P, 2, 256]),
                        op0=ALU.mult, op1=ALU.add).then_inc(s_read, 1)
                dve.wait_ge(s_read, 2 * u + 2)
                blocks = s.rearrange("p (b k) -> p b k", k=P)
                if u == 0:
                    for g in range(NKV):
                        link(dve.memset(s[:, g * 512:g * 512 + 256].rearrange("p (a k) -> p a k", a=2)[:, :, 0:PAD],
                                        NEG_INF))
                nm, sm = nmax[:, u % 2, :], smax[:, u % 2, :]
                link(dve.tensor_reduce(nm, blocks, AX.X, ALU.max))
                link(dve.scalar_tensor_tensor(out=nm, in0=nm, scalar=-1.0, in1=nsink[:, :], op0=ALU.mult,
                                              op1=ALU.min))
                dve.tensor_tensor(sm, sink[:, :], nm, ALU.add).then_inc(max_done, 1)

            def softmax_sum(u):
                dve.wait_ge(exp_done, 9 * (u + 1))
                d = den[:, u % 2, :]
                link(dve.tensor_tensor(d, d, esink[:, u % 2, :], ALU.add))
                dve.reciprocal(d, d).then_inc(den_done, 1)

            def read_o(u):
                dve.wait_ge(o_done, u + 1)
                dve.tensor_copy(qT[:, 2 * u:2 * u + 2, :, :],
                                bank[3][:, :].rearrange("p (c j q) -> p c j q", c=2, q=CHUNK)).then_inc(o_read, 1)

            def add_l(g):
                n, hf, m = g // 8, (g % 8) // 4, g % 4
                dve.wait_ge(main_done, L0 + g + 1)
                dst = xT[:, 4 * n + m, half(hf)]
                dve.tensor_tensor(dst, bank[(L0 + g) % MAIN][:, :], dst, ALU.add).then_inc(main_free, 1)

            norm_y(0)
            evac(IN_GROUPS - 2)
            dve.wait_ge(bias_in, 16)
            dve.wait_ge(y_done, LT)
            softmax_front(0)
            evac(IN_GROUPS - 1)
            low_y(0)
            softmax_sum(0)
            norm_y(1)
            low_y(1)
            softmax_front(1)
            for u in range(UNITS):
                if u >= 1:
                    read_o(u - 1)
                if u + 1 < UNITS:
                    softmax_sum(u + 1)
                add_l(2 * u)
                dve.wait_ge(pt_done, 2 * u + 2)
                if u >= 1:
                    dve.wait_ge(o_done, u)
                dve.tensor_copy(probT[:, 512:1024], bank[7][:, :]).then_inc(pt1_read, 1)
                if u + 2 < UNITS:
                    softmax_front(u + 2)
                add_l(2 * u + 1)
                if u >= 4:
                    j = u - 4
                    split_low(H_ATT + j, q_tile(j, 0), v_att[:, j:j + 1], LT + j, 0)
            read_o(UNITS - 1)
            for j in range(LT):
                split_low(H_ATT + 4 + j, q_tile(j, 1), v_att[:, j:j + 1], LT + j, 1)

            def add_a(g):
                n, hf, m = g // 8, (g % 8) // 4, g % 4
                dve.wait_ge(main_done, A0 + g + 1)
                s = scaled[:, g % 2, :]
                link(dve.tensor_tensor(s, bank[(A0 + g) % MAIN][:, :], r_mix[:, half(hf)], ALU.mult))
                dst = xT[:, 4 * n + m, half(hf)]
                dve.tensor_tensor(dst, dst, s, ALU.add).then_inc(main_free, 1)

            invert(SS_ATT, r_mix)
            for g in range(4):
                add_a(g)
            invert(SS_ATT + 1, r_mix)
            for g in range(4, 14):
                add_a(g)

            def normed(k, hf):
                i = KD * hf + k
                if i >= 4:
                    dve.wait_ge(h_ready, H_FFN + i - 3)
                dve.scalar_tensor_tensor(out=vn[:, k % 4, :], in0=xT[:, k, half(hf)], scalar=v_ffn[:, k:k + 1],
                                         in1=r_ffn[:, half(hf)], op0=ALU.mult, op1=ALU.mult).then_inc(vn_done, 1)

            def ffn_low(k, hf):
                dve.wait_ge(vn_done, KD * hf + k + 1)
                split_low(H_FFN + KD * hf + k, vn[:, k % 4, :], None, k, hf)

            invert(SS_FFN, r_ffn)
            normed(0, 0)
            normed(1, 0)
            ffn_low(0, 0)
            add_a(14)
            add_a(15)
            for k in range(2, KD):
                normed(k, 0)
                ffn_low(k - 1, 0)
            ffn_low(KD - 1, 0)
            invert(SS_FFN + 1, r_ffn)
            normed(0, 1)
            for k in range(1, KD):
                normed(k, 1)
                ffn_low(k - 1, 1)
            ffn_low(KD - 1, 1)

            dve.wait_ge(main_done, MAIN_GROUPS)
            dve.sem_inc(u_sq, RING_FREE)
            dve.sem_inc(u_ready, RING_FREE)
            with dve.Fori(0, FF_BLOCKS) as b:
                for j in range(4):
                    hf, m = j // 2, j % 2
                    dve.wait_ge(relu_done, 4 * b + (4 + j + 1))
                    dve.wait_ge(u_ready, 4 * b + (j - 1 + RING_FREE))
                    dve.tensor_tensor(usq[:, j % 2, :], relu[:, j % 2, :], relu[:, j % 2, :], ALU.mult
                                      ).then_inc(u_sq, 1)
                    dve.wait_ge(u_sq, 4 * b + (RING_FREE + j + 1))
                    dve.wait_ge(u_high, 4 * b + (j + 1))
                    dve.tensor_tensor(u_lo[:, m, half(hf)], usq[:, j % 2, :], u_hi[:, m, half(hf)],
                                      ALU.subtract).then_inc(u_ready, 1)
                for q in range(16):
                    hf, m = q // KD, q % KD
                    dve.wait_ge(ff2_done, 16 * b + (q + 1))
                    dst = xT[:, m, half(hf)]
                    dve.tensor_tensor(dst, bank[4 + q % 4][:, :], dst, ALU.add).then_inc(y_added, 1)

            for k in range(KD):
                split_low(H_PLE + k, xT[:, k, half(0)], v_ple[:, k:k + 1], k, 0)
            for i in range(4):
                k, hf = i % 2, i // 2
                dve.wait_ge(pp_high, i + 1)
                dve.tensor_tensor(pT_lo[:, k, half(hf)], bank[4 + i][:, :], pT_hi[:, k, half(hf)],
                                  ALU.subtract).then_inc(pp_ready, 1)
            invert(SS_PLE, r_mix)

            def gate_scale(q):
                hf, m = q // KD, q % KD
                dve.wait_ge(gate_done, q + 1)
                if q >= 2:
                    dve.wait_ge(x_gated, 2 * (q - 1))
                dve.tensor_tensor(gt[:, q % 2, :], bank[q % 2][:, :], r_mix[:, half(hf)], ALU.mult
                                  ).then_inc(gate_scaled, 1)

            def gate_add(q):
                hf, m = q // KD, q % KD
                dve.wait_ge(gate_sig, q + 1)
                dve.wait_ge(ple_done, q + 1)
                dve.tensor_tensor(gt[:, q % 2, :], bank[2 + q % 2][:, :], gt[:, q % 2, :], ALU.mult
                                  ).then_inc(x_gated, 1)
                dve.wait_ge(x_gated, 2 * q + 1)
                dve.tensor_tensor(xT[:, m, half(hf)], xT[:, m, half(hf)], gt[:, q % 2, :], ALU.add
                                  ).then_inc(x_gated, 1)

            def out_tile(t):
                for b in range(2):
                    dve.wait_ge(nat_done, 2 * t + b + 1)
                    if t >= 2:
                        dve.wait_ge(out_done[t % 2], 16 * (t // 2))
                    dve.scalar_tensor_tensor(out=o_nat[:, t % 2, b * HALF:(b + 1) * HALF],
                                             in0=bank[(6 if t % 2 == 0 else 4) + b][:, :],
                                             scalar=rnat[:, t:t + 1], in1=g_fin[:, b * HALF:(b + 1) * HALF],
                                             op0=ALU.mult, op1=ALU.mult).then_inc(nat_read, 1)

            dve.wait_ge(gfin_in, 16)
            for q in range(2 * KD):
                gate_scale(q)
                if q == 0:
                    for k in range(KD):
                        split_low(H_PLE + KD + k, xT[:, k, half(1)], v_ple[:, k:k + 1], k, 1)
                if q == 5:
                    invert(SS_PLE + 1, r_mix)
                if q % 2 == 1:
                    gate_add(q - 1)
                    gate_add(q)
                if q == KD + 4:
                    dve.wait_ge(rnat_root, 1)
                    link(dve.reciprocal(rnat[:, 0:4], rnat[:, 0:4]))
                if q in (KD + 5, KD + 7):
                    out_tile(q - KD - 5)
                    out_tile(q - KD - 4)
            dve.wait_ge(rnat_root, 2)
            link(dve.reciprocal(rnat[:, 4:8], rnat[:, 4:8]))
            for t in range(4, TT):
                out_tile(t)


def kernel(**inputs):
    import concourse.bacc as bacc
    from concourse.bass_utils import run_bass_kernel_spmd

    names = ["x", "p", "g_mix", "w_in", "w_conv", "b_conv", "w_lru_a", "b_lru_a", "w_lru_i", "b_lru_i",
             "lru_lambda", "sinks", "g_lru_out", "g_attn_out", "w_out", "g_ffn", "w_ff1", "w_ff2", "g_ple",
             "w_ple_gate", "w_ple_proj", "g_final"]
    arrays = {}
    for name in names:
        a = np.ascontiguousarray(inputs[name])
        if name == "p":
            a = a[0, 0]
        elif name != "g_final":
            a = a[0]
        arrays[name] = np.ascontiguousarray(a)
    head = (4 * np.arange(2)[None, :, None] + 2 * np.arange(2)[None, None, :]
            + np.repeat(np.arange(2), HD)[:, None, None])
    dist = np.abs(CHUNK + np.tile(np.arange(CHUNK), 2)[:, None] - np.arange(2 * CHUNK)[None, :])
    arrays["alibi"] = (-(2.0 ** -(head + 1.0))[:, :, :, None] * dist[:, None, None, :]).reshape(P, 512).astype(
        np.float32)
    nc = bacc.Bacc("TRN2", target_bir_lowering=False, num_devices=1, dynamic_dma_scratch_size=1024)
    args = {n: nc.dram_tensor(f"in_{n}", a.shape, mybir.dt.from_np(a.dtype), kind="ExternalInput").ap()
            for n, a in arrays.items()}
    out = nc.dram_tensor("out_x", (SEQ, D), F32, kind="ExternalOutput").ap()
    build(nc, out=out, **args)
    r = run_bass_kernel_spmd(nc, [{f"in_{n}": a for n, a in arrays.items()}], core_ids=[0])
    return r.results[0]["out_x"].reshape(1, SEQ, D)
```

```python
from contextlib import ExitStack

import numpy as np

import concourse.bass as bass
from concourse import mybir

F32 = mybir.dt.float32
F32R = mybir.dt.float32r
ALU = mybir.AluOpType
ACT = mybir.ActivationFunctionType
AX = mybir.AxisListType

P = 128
SEQ = 1024
D = 1024
KD = D // P
HALF = SEQ // 2
LRU = D // 2
LT = LRU // P
ATT = D // 2
HD = 64
NQ, NKV = 8, 2
CHUNK = 64
KVW = NKV * HD
IN_W = 2 * LRU + ATT + 2 * KVW
FF = 4 * D
PLE = 256
EPS = 1e-6
NEG_INF = -1e30
UNITS = SEQ // (2 * CHUNK)
PAD = CHUNK

PIECE = 2048
HP = PIECE // 2
STAGES = 4
IN_PIECES = IN_W // 256
OUT_PIECES = 4
FF_BLOCK = 256
FF_BLOCKS = FF // FF_BLOCK
GATE_PIECES = D // 256
FF_FIRST = IN_PIECES + OUT_PIECES
GATE_FIRST = FF_FIRST + 2 * FF_BLOCKS

IN_GROUPS = 4 * IN_PIECES
L_GROUPS = 16
A_GROUPS = 16
L0 = IN_GROUPS
A0 = L0 + L_GROUPS
MAIN_GROUPS = A0 + A_GROUPS
IN_BANKS = 4
OUT_BANKS = 3
GATE_AT = [5, 9, 13, 17]

H_MIX, H_LRU, H_ATT, H_FFN, H_PLE = 0, 16, 24, 32, 48
SS_MIX, SS_LRU, SS_ATT, SS_FFN, SS_PLE, SS_FIN = 0, 2, 4, 6, 8, 10
SQ_TILES = [8, 8, 4, 4, 4, 4, 8, 8, 8, 8, 8, 8]
SQ_BY = [sum(SQ_TILES[:n + 1]) for n in range(len(SQ_TILES))]
RING = 2
POOL_OUT, DVE_OUT = (5, 6, 7), (0, 1, 2, 3, 4)
OUT_ORDER = (0, 5, 1, 2, 6, 3, 4, 7)
RING_FREE = 2


VEC = {}
for _name, _n in (("g_mix", KD), ("w_conv", 4 * LT), ("b_conv", LT), ("b_lru_a", LT), ("b_lru_i", LT),
                  ("lru_lambda", LT), ("g_lru_out", LT), ("g_attn_out", LT), ("g_ffn", KD), ("g_ple", KD),
                  ("g_final", KD), ("sinks", 8)):
    VEC[_name] = slice(sum(v.stop - v.start for v in VEC.values()), sum(v.stop - v.start for v in VEC.values()) + _n)
NVEC = sum(v.stop - v.start for v in VEC.values())


def build(nc, x, p, vectors, gates_w, w_in, w_out, w_ff1, w_ff2, w_ple_gate, w_ple_proj, alibi, out):
    ctx = ExitStack()
    with ctx:
        KB = 1024
        base = -(-(nc.sbuf_base) // 32) * 32

        def at(name, offset, shape, dt=F32):
            return nc.alloc_sbuf_tensor_at(name, shape, dt, offset=base + offset)

        def sem(name):
            return ctx.enter_context(nc.semaphore(name))

        XT, HH, HL, WH, WL, ST = 0, 32 * KB, 64 * KB, 96 * KB, 112 * KB, 128 * KB
        T, Y, G, Q = 144 * KB, 160 * KB, 176 * KB, 192 * KB
        KV = 208 * KB
        xT = at("xT", XT, [P, KD, SEQ])
        h_hi = at("h_hi", HH, [P, KD, SEQ], F32R)
        h_lo = at("h_lo", HL, [P, KD, SEQ], F32R)
        w_hi = at("w_hi", WH, [P, 2, PIECE], F32R)
        w_lo = at("w_lo", WL, [P, 2, PIECE], F32R)
        stage = at("stage", ST, [P, STAGES, HP])
        gate_w = at("gate_w", Q, [P, 2, LT, P])
        sq = at("sq", T, [P, RING, HALF])
        acc = at("acc", T + 4 * KB, [P, SEQ])
        lru_r = at("lru_r", T, [P, SEQ])
        lru_i = at("lru_i", T + 4 * KB, [P, SEQ])
        lru_u = at("lru_u", T + 8 * KB, [P, SEQ])
        lru_x = at("lru_x", T + 12 * KB, [P, SEQ])
        yl = at("yl", Y, [P, LT, SEQ])
        gl = at("gl", G, [P, LT, SEQ])
        r_lru = at("r_lru", G + 4 * KB, [P, SEQ])
        qT = at("qT", Q, [P, SEQ // CHUNK, LT, CHUNK])
        kT = at("kT", KV, [P, PAD + SEQ])
        vT = at("vT", KV + 4 * (PAD + SEQ), [P, PAD + SEQ])
        v_win = at("v_win", T + 8 * KB, [P, SEQ // CHUNK, P])
        prob = at("prob", G, [P, 2, 1024])
        probT = at("probT", G + 8 * KB, [P, 1024])
        bias = at("bias", G + 12 * KB, [P, 512])
        scaled = at("scaled", T + 8 * KB, [P, 2, HALF])
        r_ffn = at("r_ffn", KV, [P, SEQ])
        u_hi = at("u_hi", Y, [P, 2, SEQ], F32R)
        u_lo = at("u_lo", Y + 8 * KB, [P, 2, SEQ], F32R)
        relu = at("relu", G, [P, 2, HALF])
        usq = at("usq", G + 4 * KB, [P, 2, HALF])
        pT = at("pT", G + 8 * KB, [P, 2, SEQ])
        pT_hi = at("pT_hi", T, [P, 2, SEQ], F32R)
        pT_lo = at("pT_lo", T + 8 * KB, [P, 2, SEQ], F32R)
        pw_hi = at("pw_hi", Q, [P, PIECE], F32R)
        pw_lo = at("pw_lo", Q + 8 * KB, [P, PIECE], F32R)
        gt = at("gt", G, [P, 2, HALF])
        r_fin = at("r_fin", KV, [P, SEQ])
        sq2 = at("sq2", G + 4 * KB, [P, RING, HALF])
        acc2 = at("acc2", KV + 4 * (PAD + SEQ), [P, SEQ])
        o_ring = at("o_ring", Y, [P, KD, HALF])
        at_byte = KV + 2 * 4 * (PAD + SEQ)
        small = {}
        for name, shape in (("r_mix", [P, SEQ]), ("ident", [P, P]), ("ones", [P, P]), ("vec", [P, NVEC]),
                            ("nsink", [P, 8]), ("eps", [P, 1]),
                            ("lam", [P, 6, LT]), ("nmax", [P, 2, 8]), ("smax", [P, 2, 8]),
                            ("esink", [P, 2, 8]), ("den", [P, 2, 8])):
            small[name] = at(name, at_byte, shape)
            at_byte += -(-4 * int(np.prod(shape[1:])) // 32) * 32
        r_mix, ident, ones, vec = (small[n] for n in ("r_mix", "ident", "ones", "vec"))
        nsink, eps, lam = (small[n] for n in ("nsink", "eps", "lam"))
        nmax, smax, esink, den = (small[n] for n in ("nmax", "smax", "esink", "den"))
        (v_mix, v_conv, v_bconv, v_ba, v_bi, v_lam, v_lru, v_att, v_ffn, v_ple, v_fin, sink) = (
            vec[:, VEC[n]] for n in VEC)
        c_tanh, c_exp = lam[:, 4, :], lam[:, 5, :]

        bank = [ctx.enter_context(nc.psum_tensor(f"bank{i}", [P, HALF], F32)) for i in range(8)]

        x_in = [sem(f"x_in{i}") for i in range(8)]
        stage_in = [sem(f"stage_in{i}") for i in range(STAGES)]
        vec_in, gatew_in, bias_in, p_in = sem("vec_in"), sem("gatew_in"), sem("bias_in"), sem("p_in")
        out_ready = [sem(f"out_ready{k}") for k in range(KD)]
        out_done = [sem(f"out_done{k}") for k in range(KD)]
        consts, w_split, sq_used, p_ready, pool_chain = (
            sem(n) for n in ("consts", "w_split", "sq_used", "p_ready", "pool_chain"))
        main_done, gates_done, ss_done, vt_done, s_done, pt_done, o_done, ff1_done, ff2_done, gate_done, ple_done = (
            sem(n) for n in ("main_done", "gates_done", "ss_done", "vt_done", "s_done", "pt_done", "o_done",
                             "ff1_done", "ff2_done", "gate_done", "ple_done"))
        w_high, h_high, sq_done, rms_done, lam_exp, gates_sig, lru_tanh, lru_exp, lru_root = (
            sem(n) for n in ("w_high", "h_high", "sq_done", "rms_done", "lam_exp", "gates_sig", "lru_tanh",
                             "lru_exp", "lru_root"))
        gelu_done, vt_read, exp_done, pt0_read, u_high, pp_high, gate_sig, x_scaled = (
            sem(n) for n in ("gelu_done", "vt_read", "exp_done", "pt0_read", "u_high", "pp_high", "gate_sig",
                             "x_scaled"))
        dve_chain, lam_abs, lam_ready, h_ready, main_free, conv_done, lru_m2, state_done = (
            sem(n) for n in ("dve_chain", "lam_abs", "lam_ready", "h_ready", "main_free", "conv_done", "lru_m2",
                             "state_done"))
        y_done, y_normed, s_read, max_done, den_done, pt1_read, o_read, pads_ready = (
            sem(n) for n in ("y_done", "y_normed", "s_read", "max_done", "den_done", "pt1_read", "o_read",
                             "pads_ready"))
        relu_done, u_sq, u_ready, y_added, pp_ready, gate_scaled, x_gated, fin_ready = (
            sem(n) for n in ("relu_done", "u_sq", "u_ready", "y_added", "pp_ready", "gate_scaled", "x_gated",
                             "fin_ready"))

        def half(hf):
            return slice(hf * HALF, (hf + 1) * HALF)

        def ffn_number(k, hf):
            return H_FFN + 8 * (k // 4) + 4 * hf + k % 4

        def q_tile(j, hf):
            return qT[:, hf * 8:(hf + 1) * 8, j, :]

        def by_chunk(ap):
            return ap.rearrange("p (c q) -> p c q", q=CHUNK)

        def slot(n):
            return (n - (n > GATE_FIRST)) % 2

        def main_bank(g):
            if g < L0:
                return bank[g % IN_BANKS], g - IN_BANKS if g >= IN_BANKS else None
            i = (g - L0) % OUT_BANKS
            if g - L0 < OUT_BANKS:
                return bank[i], max(q for q in range(L0) if q % IN_BANKS == i)
            return bank[i], g - OUT_BANKS

        def piece_free(eng, n):
            if n < IN_PIECES:
                eng.wait_ge(main_done, 4 * (n + 1))
            else:
                eng.wait_ge(main_done, IN_GROUPS + 8 * (n - IN_PIECES + 1))

        def add_square(eng, n, i, ring, total):
            q = SQ_BY[n] - SQ_TILES[n] + i
            if n >= 2 and i == 0:
                eng.wait_ge(ss_done, n - 1)
            eng.wait_ge(sq_done, q + 1)
            if q >= 1:
                eng.wait_ge(sq_used, q)
            dst, src = total[:, half(n % 2)], ring[:, q % RING, :]
            if i == 0:
                eng.tensor_copy(dst, src).then_inc(sq_used, 1)
            else:
                eng.tensor_tensor(dst, dst, src, ALU.add).then_inc(sq_used, 1)

        block = ctx.enter_context(nc.Block())

        @block.sync
        def _(sp):
            def load_x(i):
                hf, k = i // 4, 2 * (i % 4)
                sp.dma_start(xT[:, k:k + 2, half(hf)], x.rearrange("(k p) t -> p k t", p=P)[:, k:k + 2, half(hf)]
                             ).then_inc(x_in[i], 16)

            def load_half(s, src):
                if s >= STAGES:
                    sp.wait_ge(w_split, s - STAGES + 1)
                sp.dma_start(stage[:, s % STAGES, :], src).then_inc(stage_in[s % STAGES], 16)

            def load_piece(n, w, i):
                for h in range(2):
                    load_half(2 * n + h, w[i, h])

            sp.dma_start(vec[:, :], vectors).then_inc(vec_in, 16)
            load_x(0)
            load_half(0, w_in[0, 0])
            load_x(1)
            load_x(2)
            load_half(1, w_in[0, 1])
            for i in range(3, 8):
                load_x(i)
            for n in range(1, IN_PIECES):
                load_piece(n, w_in, n)
                if n == 1:
                    sp.dma_start(gate_w[:, :, :, :], gates_w).then_inc(gatew_in, 16)
            load_piece(IN_PIECES, w_out, 0)
            sp.wait_ge(y_done, LT)
            sp.dma_start(bias[:, :], alibi).then_inc(bias_in, 16)
            for i in range(1, OUT_PIECES):
                load_piece(IN_PIECES + i, w_out, i)
            with sp.Fori(0, FF_BLOCKS) as b:
                for i in range(4):
                    s0 = 2 * FF_FIRST + i
                    sp.wait_ge(w_split, 4 * b + (s0 - STAGES + 1))
                    sp.dma_start(stage[:, s0 % STAGES, :], (w_ff1 if i < 2 else w_ff2)[b, i % 2]
                                 ).then_inc(stage_in[s0 % STAGES], 16)
            for i in range(9):
                if i == 1:
                    load_piece(GATE_FIRST + i, w_ple_proj, 0)
                else:
                    load_piece(GATE_FIRST + i, w_ple_gate, (0 if i == 0 else i - 1) % GATE_PIECES)
            for hf in range(2):
                for k in range(KD) if hf == 0 else OUT_ORDER:
                    sp.wait_ge(out_ready[k], hf + 1)
                    sp.dma_start(out[k * P:(k + 1) * P, half(hf)], o_ring[:, k, :]).then_inc(out_done[k], 16)
            for k in range(KD):
                sp.wait_ge(out_done[k], 2 * 16)

        @block.gpsimd
        def _(pool):
            pool.memset(ident[:, :], 0.0).then_inc(pool_chain, 1)
            pool.memset(ones[:, :], 1.0).then_inc(consts, 1)
            pool.memset(eps[:, :], EPS).then_inc(consts, 1)
            pool.wait_ge(pool_chain, 1)
            pool.affine_select(out=ident[:, :], in_=ident[:, :], compare_op=ALU.not_equal, fill=1.0,
                               base=0, pattern=[[-1, P]], channel_multiplier=1).then_inc(consts, 1)

            def low(s, dst=None):
                n = s // 2
                pool.wait_ge(w_high, s + 1)
                o = (s % 2) * HP
                lo, hi = (w_lo[:, slot(n), o:o + HP], w_hi[:, slot(n), o:o + HP]) if dst is None else dst
                pool.tensor_tensor(lo, stage[:, s % STAGES, :], hi, ALU.subtract).then_inc(w_split, 1)

            def sums(n, ring, total):
                for i in range(SQ_TILES[n]):
                    add_square(pool, n, i, ring, total)

            def probs(u):
                pool.wait_ge(den_done, u + 1)
                e = prob[:, u % 2, :].rearrange("p (b k) -> p b k", k=P)
                pool.tensor_tensor(e, e, den[:, u % 2, :].unsqueeze(2).to_broadcast([P, 8, P]),
                                   ALU.mult).then_inc(p_ready, 1)

            for s in range(4):
                low(s)
            sums(SS_MIX + 1, sq, acc)
            for n in range(2, IN_PIECES):
                low(2 * n)
                low(2 * n + 1)
                if n == 5:
                    sums(SS_LRU, sq, acc)
                    sums(SS_LRU + 1, sq, acc)
            low(2 * 7)
            low(2 * 7 + 1)
            probs(0)
            probs(1)
            low(2 * 8)
            low(2 * 8 + 1)
            for p_ in range(8):
                if p_ == 4:
                    low(2 * 9)
                    low(2 * 9 + 1)
                if p_ + 2 < UNITS:
                    probs(p_ + 2)
            sums(SS_ATT, sq, acc)
            low(2 * 10)
            low(2 * 10 + 1)
            sums(SS_ATT + 1, sq, acc)
            sums(SS_FFN, sq, acc)
            low(2 * FF_FIRST)
            low(2 * FF_FIRST + 1)
            sums(SS_FFN + 1, sq, acc)
            with pool.Fori(0, FF_BLOCKS) as b:
                for i in range(4):
                    s0 = 2 * FF_FIRST + 2 + i
                    n0, o = s0 // 2, (s0 % 2) * HP
                    pool.wait_ge(w_high, 4 * b + (s0 + 1))
                    pool.tensor_tensor(w_lo[:, n0 % 2, o:o + HP], stage[:, s0 % STAGES, :],
                                       w_hi[:, n0 % 2, o:o + HP], ALU.subtract).then_inc(w_split, 1)
            sums(SS_PLE, sq2, acc2)
            s0 = 2 * (GATE_FIRST + 1)
            for s in (s0, s0 + 1):
                o = (s % 2) * HP
                low(s, (pw_lo[:, o:o + HP], pw_hi[:, o:o + HP]))
            low(s0 + 2)
            low(s0 + 3)
            sums(SS_PLE + 1, sq2, acc2)
            for q in range(2 * KD):
                if q >= 2:
                    add_square(pool, SS_FIN + (q - 2) // KD, (q - 2) % KD, sq2, acc2)
                if q % 2 == 1 and q // 2 < 6:
                    low(2 * (GATE_FIRST + 3 + q // 2))
                    low(2 * (GATE_FIRST + 3 + q // 2) + 1)
            add_square(pool, SS_FIN + 1, KD - 2, sq2, acc2)
            pool.wait_ge(x_scaled, KD)
            pool.wait_ge(fin_ready, 1)
            for k in POOL_OUT:
                pool.wait_ge(out_done[k], 16)
                pool.tensor_tensor(o_ring[:, k, :], xT[:, k, half(1)], r_fin[:, half(1)], ALU.mult
                                   ).then_inc(out_ready[k], 1)

        @block.tensor
        def _(pe):
            def passes(o, whi, wlo, hh, hl, first, last):
                pe.matmul(o, whi, hh, start=first, stop=False)
                pe.matmul(o, whi, hl, start=False, stop=False)
                return pe.matmul(o, wlo, hh, start=False, stop=last)

            def group(g, n, kt, m, hf, k_h, h_first, ready):
                cols = PIECE // kt
                o, before = main_bank(g)
                o = o[:, :]
                if before is not None:
                    pe.wait_ge(main_free, before + 1)
                for k in range(kt):
                    if ready and k == 0:
                        pe.wait_ge(w_split, 2 * n + 1)
                    if ready and k == kt // 2:
                        pe.wait_ge(w_split, 2 * n + 2)
                    if h_first is not None:
                        pe.wait_ge(h_ready, h_first + k + 1)
                    c = k * cols + m * P
                    sl = [w[:, n % 2, c:c + P] for w in (w_hi, w_lo)]
                    hh, hl = h_hi[:, k_h + k, half(hf)], h_lo[:, k_h + k, half(hf)]
                    last = passes(o, sl[0], sl[1], hh, hl, k == 0, k == kt - 1)
                last.then_inc(main_done, 1)

            def first_groups(hf):
                g = 2 * hf
                for k in range(KD):
                    if hf == 0 and k % 4 == 0:
                        pe.wait_ge(w_split, 1 + k // 4)
                    pe.wait_ge(h_ready, H_MIX + 8 * hf + k + 1)
                    for m in range(2):
                        c = k * 256 + m * P
                        last = passes(bank[g + m][:, :], w_hi[:, 0, c:c + P], w_lo[:, 0, c:c + P],
                                      h_hi[:, k, half(hf)], h_lo[:, k, half(hf)], k == 0, k == KD - 1)
                        if k == KD - 1:
                            last.then_inc(main_done, 1)
                    if hf == 1 and k == 1:
                        sum_rows(SS_MIX, acc, 7)

            def sum_rows(n, total, b):
                pe.wait_ge(sq_used, SQ_BY[n])
                if n >= 1:
                    pe.wait_ge(rms_done, n)
                pe.matmul(bank[b][:, :], ones[:, :], total[:, half(n % 2)], start=True, stop=True
                          ).then_inc(ss_done, 1)

            def gates(j):
                pe.wait_ge(gatew_in, 16)
                pe.wait_ge(conv_done, j + 1)
                for hf in range(2):
                    for i in range(2):
                        b = 4 + 2 * hf + i
                        if j >= 1:
                            pe.wait_ge(gates_sig, 4 * (j - 1) + 2 * hf + i + 1)
                        else:
                            pe.wait_ge(rms_done, SS_MIX + 2)
                        pe.matmul(bank[b][:, :], gate_w[:, i, j, :], lru_x[:, half(hf)], start=True, stop=True
                                  ).then_inc(gates_done, 1)

            def turn_v(i):
                pe.wait_ge(main_free, 4 * 4 + 4)
                pe.wait_ge(pads_ready, 2)
                if i >= 2:
                    pe.wait_ge(vt_read, i - 1)
                else:
                    pe.wait_ge(gates_sig, 16)
                for c in range(4 * i, 4 * i + 4):
                    last = pe.transpose(bank[6 + i % 2][:, (c % 4) * P:(c % 4 + 1) * P],
                                        vT[:, c * CHUNK:c * CHUNK + P], ident[:, :])
                last.then_inc(vt_done, 1)

            def scores(u):
                pe.wait_ge(main_free, IN_GROUPS - 2 + (2 if u >= UNITS // 2 else 0))
                for g in range(NKV):
                    if u >= 1:
                        pe.wait_ge(s_read, 2 * (u - 1) + g + 1)
                    else:
                        pe.wait_ge(rms_done, SS_LRU + 2)
                    r = slice(g * HD, (g + 1) * HD)
                    for cp in range(2):
                        c = 2 * u + cp
                        for a in range(2):
                            last = pe.matmul(bank[4 + g][:, (2 * cp + a) * P:(2 * cp + a + 1) * P],
                                             qT[r, c, 2 * a:2 * a + 2, :].rearrange("p a q -> p (a q)"),
                                             kT[r, c * CHUNK:c * CHUNK + P], start=True, stop=True)
                    last.then_inc(s_done, 1)

            def turn_p(u):
                pe.wait_ge(p_ready, u + 1)
                for g in range(NKV):
                    if u >= 1:
                        pe.wait_ge(pt0_read if g == 0 else pt1_read, u)
                    else:
                        pe.wait_ge(vt_read, 4)
                    for i in range(4):
                        last = pe.transpose(bank[6 + g][:, i * P:(i + 1) * P],
                                            prob[:, u % 2, (4 * g + i) * P:(4 * g + i + 1) * P], ident[:, :])
                    last.then_inc(pt_done, 1)

            def values(u):
                pe.wait_ge(pt0_read, u + 1)
                pe.wait_ge(pt1_read, u + 1)
                if u >= 1:
                    pe.wait_ge(o_read, u)
                else:
                    pe.wait_ge(main_free, L0)
                for cp in range(2):
                    for g in range(NKV):
                        last = pe.matmul(bank[3][g * HD:(g + 1) * HD, cp * 256:(cp + 1) * 256],
                                         v_win[:, 2 * u + cp, g * HD:(g + 1) * HD],
                                         probT[:, g * 512 + cp * 256:g * 512 + (cp + 1) * 256],
                                         start=True, stop=True)
                last.then_inc(o_done, 1)

            pe.wait_ge(consts, 3)
            first_groups(0)
            first_groups(1)
            sum_rows(SS_MIX + 1, acc, 7)
            for g in range(4, IN_GROUPS):
                n, hf, m = g // 4, (g % 4) // 2, g % 2
                group(g, n, KD, m, hf, 0, None, g % 4 == 0)
                if g in GATE_AT:
                    gates(GATE_AT.index(g))
                if g in (22, 23):
                    sum_rows(SS_LRU + g - 22, acc, 5)
                if 21 <= g < 25:
                    turn_v(g - 21)
                if g == 26:
                    scores(0)
            scores(1)
            for u in range(UNITS):
                for i in range(2):
                    g = 2 * u + i
                    n, hf, m = g // 8, (g % 8) // 4, g % 4
                    group(L0 + g, IN_PIECES + n, LT, m, hf, 0, H_LRU + 4 * hf if n == 0 and m == 0 else None,
                          g % 8 == 0)
                    if i == 0:
                        turn_p(u)
                        if u + 2 < UNITS:
                            scores(u + 2)
                if u == UNITS - 1:
                    pe.wait_ge(s_read, 2 * UNITS)
                    sum_rows(SS_ATT, acc, 4)
                values(u)
            for g in range(A_GROUPS):
                n, hf, m = g // 8, (g % 8) // 4, g % 4
                group(A0 + g, IN_PIECES + 2 + n, LT, m, hf, LT, H_ATT + 4 * hf if n == 0 and m == 0 else None,
                      g % 8 == 0)
                if g == 2:
                    sum_rows(SS_ATT + 1, acc, 5)
                if g == 14:
                    sum_rows(SS_FFN, acc, 7)

            n1, n2 = FF_FIRST % 2, (FF_FIRST + 1) % 2

            def ff1(b, hf, m):
                j = 2 * hf + m
                if j == 0:
                    pe.wait_ge(w_split, 4 * b + 2 * (FF_FIRST + 1))
                pe.wait_ge(relu_done, 4 * b + (j + 1))
                for k in range(KD):
                    c = k * 256 + m * P
                    hh, hl = h_hi[:, k, half(hf)], h_lo[:, k, half(hf)]
                    last = passes(bank[j][:, :], w_hi[:, n1, c:c + P], w_lo[:, n1, c:c + P], hh, hl,
                                  k == 0, k == KD - 1)
                last.then_inc(ff1_done, 1)

            def ff2(b):
                pe.wait_ge(w_split, 4 * b + 2 * (FF_FIRST + 2))
                for hf in range(2):
                    pe.wait_ge(u_ready, 4 * b + (2 * hf + 2 + RING_FREE))
                    for m in range(KD):
                        q = KD * hf + m
                        o = bank[4 + q % 4][:, :]
                        pe.wait_ge(y_added, 16 * b + (q + 1))
                        for k in range(2):
                            c = k * D + m * P
                            hh, hl = u_hi[:, k, half(hf)], u_lo[:, k, half(hf)]
                            last = passes(o, w_hi[:, n2, c:c + P], w_lo[:, n2, c:c + P], hh, hl, k == 0, k == 1)
                        last.then_inc(ff2_done, 1)

            pe.sem_inc(relu_done, 4)
            pe.sem_inc(y_added, 4)
            pe.wait_ge(rms_done, SS_ATT + 2)
            pe.wait_ge(o_read, UNITS)
            for hf in range(2):
                pe.wait_ge(h_ready, ffn_number(KD - 1, hf) + 1)
                for m in range(2):
                    if hf == 0:
                        pe.wait_ge(main_free, MAIN_GROUPS - 1 + m)
                    ff1(0, hf, m)
                    if hf == 1 and m == 0:
                        sum_rows(SS_FFN + 1, acc, 7)
            pe.wait_ge(rms_done, SS_FFN + 2)
            ff2(0)
            with pe.Fori(1, FF_BLOCKS) as b:
                for hf in range(2):
                    for m in range(2):
                        ff1(b, hf, m)
                ff2(b)

            pe.wait_ge(relu_done, 4 + 4 * FF_BLOCKS)

            def gate(hf, i, m):
                n = GATE_FIRST + (0 if hf == 0 and i == 0 else 1 + i + 4 * hf)
                q = KD * hf + 2 * i + m
                if q >= 2:
                    pe.wait_ge(gate_scaled, q - 1)
                if m == 0:
                    pe.wait_ge(w_split, 2 * n + 2)
                for k in range(KD):
                    if i == 0 and m == 0:
                        pe.wait_ge(h_ready, H_PLE + 8 * hf + k + 1)
                    c = k * 256 + m * P
                    hh, hl = h_hi[:, k, half(hf)], h_lo[:, k, half(hf)]
                    o = bank[q % 2][:, :]
                    last = passes(o, w_hi[:, slot(n), c:c + P], w_lo[:, slot(n), c:c + P], hh, hl, k == 0, k == KD - 1)
                last.then_inc(gate_done, 1)

            def project(hf, m):
                q = KD * hf + m
                if q == 0:
                    pe.wait_ge(w_split, 2 * (GATE_FIRST + 1) + 2)
                if m == 0:
                    pe.wait_ge(pp_ready, 2 * hf + 2)
                if q >= 2:
                    pe.wait_ge(x_gated, 2 * (q - 2) + 1)
                for k in range(2):
                    c = k * D + m * P
                    hh, hl = pT_hi[:, k, half(hf)], pT_lo[:, k, half(hf)]
                    o = bank[2 + q % 2][:, :]
                    last = passes(o, pw_hi[:, c:c + P], pw_lo[:, c:c + P], hh, hl, k == 0, k == 1)
                last.then_inc(ple_done, 1)

            for hf in range(2):
                for i in range(GATE_PIECES):
                    for m in range(2):
                        gate(hf, i, m)
                        if hf == 0 and i == 0 and m == 0:
                            pe.wait_ge(y_added, 4 + 16 * FF_BLOCKS)
                            sum_rows(SS_PLE, acc2, 4)
                    for m in range(2):
                        project(hf, 2 * i + m)
                    if hf == 0 and i == 1:
                        sum_rows(SS_PLE + 1, acc2, 4)
                    if hf == 1 and i == 1:
                        sum_rows(SS_FIN, acc2, 4)
            n = SS_FIN + 1
            pe.wait_ge(sq_used, SQ_BY[n] - 1)
            pe.wait_ge(rms_done, n)
            pe.matmul(bank[4][:, :], ones[:, :], acc2[:, half(1)], start=True, stop=False)
            pe.wait_ge(sq_done, SQ_BY[n])
            pe.matmul(bank[4][:, :], ones[:, :], sq2[:, (SQ_BY[n] - 1) % RING, :], start=False, stop=True
                      ).then_inc(ss_done, 1)

        @block.scalar
        def _(act):
            def high(s, dst=None):
                n = s // 2
                act.wait_ge(stage_in[s % STAGES], stage_count(s))
                o = (s % 2) * HP
                hi = w_hi[:, slot(n), o:o + HP] if dst is None else dst
                act.activation(hi, stage[:, s % STAGES, :], ACT.Copy).then_inc(w_high, 1)

            def stage_count(s):
                return 16 * (s // STAGES + 1)

            def split_high(i, src, scale, k, hf):
                dst = h_hi[:, k, half(hf)]
                if H_ATT <= i < H_FFN:
                    dst = by_chunk(dst)
                if scale is None:
                    act.activation(dst, src, ACT.Copy).then_inc(h_high, 1)
                else:
                    act.activation(dst, src, ACT.Copy, scale=scale).then_inc(h_high, 1)

            def square(q, ring, src):
                if q >= RING:
                    act.wait_ge(sq_used, q - RING + 1)
                dst = ring[:, q % RING, :]
                if SQ_BY[SS_LRU + 1] <= q < SQ_BY[SS_ATT + 1]:
                    dst = by_chunk(dst)
                act.activation(dst, src, ACT.Square).then_inc(sq_done, 1)

            def root(n, b, dst, width):
                act.wait_ge(ss_done, n + 1)
                act.activation(dst[:, half(n % 2)], bank[b][:, :], ACT.Sqrt, bias=eps[:, 0:1],
                               scale=1.0 / width).then_inc(rms_done, 1)

            act.wait_ge(consts, 3)
            act.activation(lam[:, 2, :], ones[:, 0:LT], ACT.Square)
            act.wait_ge(vec_in, 16)
            for hf in range(2):
                for k in range(KD):
                    if k % 2 == 0:
                        act.wait_ge(x_in[4 * hf + k // 2], 16)
                    split_high(H_MIX + KD * hf + k, xT[:, k, half(hf)], v_mix[:, k:k + 1], k, hf)
                    square(KD * hf + k, sq, xT[:, k, half(hf)])
                    if hf == 0 and k in (1, 4):
                        high(k // 4)
                    if hf == 1 and k == 3:
                        root(SS_MIX, 7, r_mix, D)
                if hf == 0:
                    high(2)
                    high(3)
            root(SS_MIX + 1, 7, r_mix, D)
            act.wait_ge(lam_abs, 1)
            act.activation(lam[:, 1, :], lam[:, 0, :], ACT.Exp, scale=-1.0).then_inc(lam_exp, 1)

            def lru_gates(j):
                if j >= 1:
                    act.wait_ge(state_done, j)
                for hf in range(2):
                    for i, (dst, bv) in enumerate(((lru_r, v_ba), (lru_i, v_bi))):
                        act.wait_ge(gates_done, 4 * j + 2 * hf + i + 1)
                        act.activation(dst[:, half(hf)], bank[4 + 2 * hf + i][:, :], ACT.Sigmoid,
                                       bias=bv[:, j:j + 1]).then_inc(gates_sig, 1)
                act.wait_ge(lam_ready, 1)
                act.wait_ge(gates_sig, 4 * j + 4)
                act.activation(lru_u[:, :], lru_r[:, :], ACT.Tanh, scale=c_tanh[:, j:j + 1]).then_inc(lru_tanh, 1)
                act.wait_ge(lru_tanh, j + 1)
                act.activation(lru_r[:, :], lru_r[:, :], ACT.Exp, scale=c_exp[:, j:j + 1]).then_inc(lru_exp, 1)

            for g in range(IN_GROUPS):
                P_, r = g // 4, g % 4
                if r == 0 and P_ >= 1:
                    n = P_ + 1
                    piece_free(act, n - 2)
                    high(2 * n)
                    high(2 * n + 1)
                if g in GATE_AT:
                    lru_gates(GATE_AT.index(g))
                if g - 1 in GATE_AT:
                    j = GATE_AT.index(g - 1)
                    act.wait_ge(lru_m2, j + 1)
                    act.activation(lru_u[:, :], lru_u[:, :], ACT.Sqrt).then_inc(lru_root, 1)
                if g in (15, 18):
                    for j in (2 * (g == 18), 2 * (g == 18) + 1):
                        act.wait_ge(main_free, 12 if g == 15 else 16)
                        act.activation(gl[:, j, :], gl[:, j, :], ACT.Gelu_apprx_tanh).then_inc(gelu_done, 1)
                if g in (20, 21):
                    hf = g - 20
                    act.wait_ge(state_done, LT)
                    for j in range(LT):
                        act.wait_ge(y_done, j + 1)
                        square(SQ_BY[SS_LRU + hf] - 4 + j, sq, yl[:, j, half(hf)])
                if g in (22, 23):
                    root(SS_LRU + g - 22, 5, r_lru, LRU)
                if 21 <= g < 25:
                    i = g - 21
                    act.wait_ge(vt_done, i + 1)
                    act.wait_ge(state_done, LT)
                    act.activation(v_win[:, 4 * i:4 * i + 4, :], bank[6 + i % 2][:, :].rearrange(
                        "p (c d) -> p c d", d=P), ACT.Copy).then_inc(vt_read, 1)

            def exps(u):
                act.wait_ge(max_done, u + 1)
                for i in range(8):
                    e = prob[:, u % 2, i * P:(i + 1) * P]
                    act.activation(e, e, ACT.Exp, bias=nmax[:, u % 2, i:i + 1],
                                   accum_out=den[:, u % 2, i:i + 1]).then_inc(exp_done, 1)
                act.activation(esink[:, u % 2, :], smax[:, u % 2, :], ACT.Exp).then_inc(exp_done, 1)

            def lru_high(hf):
                act.wait_ge(main_done, IN_GROUPS - 2 + 2 * hf)
                for j in range(LT):
                    act.wait_ge(y_normed, 4 * hf + j + 1)
                    split_high(H_LRU + 4 * hf + j, yl[:, j, half(hf)], None, j, hf)

            lru_high(0)
            exps(0)
            lru_high(1)
            exps(1)
            piece_free(act, 6)
            high(2 * 8)
            high(2 * 8 + 1)
            for u in range(UNITS):
                act.wait_ge(pt_done, 2 * u + 1)
                if u >= 1:
                    act.wait_ge(o_done, u)
                act.activation(probT[:, 0:512], bank[6][:, :], ACT.Copy).then_inc(pt0_read, 1)
                if u == 4:
                    piece_free(act, 7)
                    high(2 * 9)
                    high(2 * 9 + 1)
                if u + 2 < UNITS:
                    exps(u + 2)
                if u in (5, 6):
                    for j in (2 * (u - 5), 2 * (u - 5) + 1):
                        split_high(H_ATT + j, q_tile(j, 0), v_att[:, j:j + 1], LT + j, 0)
                        square(SQ_BY[SS_ATT] - 4 + j, sq, q_tile(j, 0))
            root(SS_ATT, 4, r_mix, ATT)
            piece_free(act, 8)
            high(2 * 10)
            high(2 * 10 + 1)
            act.wait_ge(o_read, UNITS)
            for j in range(LT):
                split_high(H_ATT + 4 + j, q_tile(j, 1), v_att[:, j:j + 1], LT + j, 1)
            for j in range(LT):
                square(SQ_BY[SS_ATT + 1] - 4 + j, sq, q_tile(j, 1))
            root(SS_ATT + 1, 5, r_mix, ATT)
            act.dma_start(pT[:, :, :], p.rearrange("(k q) t -> q k t", q=P)).then_inc(p_in, 16)

            def ffn_high(k, hf):
                act.wait_ge(main_free, A0 + 8 * (k // 4) + 4 * hf + k % 4 + 1)
                if k == 0:
                    act.wait_ge(main_done, A0)
                if k == 4:
                    act.wait_ge(main_done, MAIN_GROUPS - 4 + 4 * hf)
                split_high(ffn_number(k, hf), xT[:, k, half(hf)], v_ffn[:, k:k + 1], k, hf)

            def ffn_square(k, hf):
                act.wait_ge(main_free, A0 + 8 * (k // 4) + 4 * hf + k % 4 + 1)
                square(SQ_BY[SS_FFN + hf] - 8 + k, sq, xT[:, k, half(hf)])

            for k in range(4):
                ffn_square(k, 0)
                ffn_high(k, 0)
            piece_free(act, 9)
            high(2 * FF_FIRST)
            high(2 * FF_FIRST + 1)
            for k in range(4):
                ffn_high(k, 1)
            for k in range(4, KD):
                ffn_square(k, 0)
                ffn_high(k, 0)
            for k in range(4):
                ffn_square(k, 1)
            root(SS_FFN, 7, r_ffn, D)
            for k in range(4, KD):
                ffn_high(k, 1)
                ffn_square(k, 1)

            def ff_high(b, i):
                s0 = 2 * FF_FIRST + 2 + i
                n0, o = s0 // 2, (s0 % 2) * HP
                act.wait_ge(stage_in[s0 % STAGES], 16 * b + stage_count(s0))
                act.activation(w_hi[:, n0 % 2, o:o + HP], stage[:, s0 % STAGES, :], ACT.Copy).then_inc(w_high, 1)

            def ff_block(b, first):
                act.wait_ge(y_added, 16 * b + 4)
                ff_high(b, 0)
                ff_high(b, 1)
                for j in range(4):
                    hf, m = j // 2, j % 2
                    if first and j == 2:
                        root(SS_FFN + 1, 7, r_ffn, D)
                    act.wait_ge(relu_done, 4 * b + (4 + j + 1))
                    act.activation(u_hi[:, m, half(hf)], relu[:, j % 2, :], ACT.Square).then_inc(u_high, 1)
                ff_high(b, 2)
                ff_high(b, 3)

            ff_block(0, True)
            act.wait_ge(p_in, 16)
            for i in range(4):
                k, hf = i % 2, i // 2
                act.activation(pT_hi[:, k, half(hf)], pT[:, k, half(hf)], ACT.Copy).then_inc(pp_high, 1)
            with act.Fori(1, FF_BLOCKS) as b:
                ff_block(b, False)

            def ple_high(hf):
                for k in range(KD):
                    act.wait_ge(y_added, 4 + 16 * (FF_BLOCKS - 1) + KD * hf + k + 1)
                    split_high(H_PLE + KD * hf + k, xT[:, k, half(hf)], v_ple[:, k:k + 1], k, hf)
                    square(SQ_BY[SS_PLE + hf] - 8 + k, sq2, xT[:, k, half(hf)])

            def project_high():
                s0 = 2 * (GATE_FIRST + 1)
                for s in (s0, s0 + 1):
                    high(s, pw_hi[:, (s % 2) * HP:(s % 2 + 1) * HP])

            def gate_high(n):
                high(2 * n)
                high(2 * n + 1)

            ple_high(0)
            project_high()
            act.wait_ge(ff2_done, 16 * FF_BLOCKS)
            gate_high(GATE_FIRST + 2)
            root(SS_PLE, 4, r_mix, D)
            ple_high(1)

            def sigmoid(q):
                act.wait_ge(gate_scaled, q + 1)
                act.activation(gt[:, q % 2, :], gt[:, q % 2, :], ACT.Sigmoid).then_inc(gate_sig, 1)

            def final_square(q):
                hf, k = q // KD, q % KD
                act.wait_ge(x_gated, 2 * (q + 1))
                square(SQ_BY[SS_FIN + hf] - 8 + k, sq2, xT[:, k, half(hf)])

            def final_scale(q):
                act.wait_ge(sq_done, SQ_BY[SS_FIN] + q - KD + 1)
                act.activation(xT[:, q - KD, half(1)], xT[:, q - KD, half(1)], ACT.Copy,
                               scale=v_fin[:, q - KD:q - KD + 1]).then_inc(x_scaled, 1)

            for q in range(2 * KD):
                sigmoid(q)
                if q >= 2:
                    final_square(q - 2)
                if q >= KD + 2:
                    final_scale(q - 2)
                if q % 2 == 1 and q // 2 < 6:
                    act.wait_ge(gate_done, q + 1)
                    gate_high(GATE_FIRST + 3 + q // 2)
                if q == 4:
                    root(SS_PLE + 1, 4, r_mix, D)
                if q == KD + 3:
                    root(SS_FIN, 4, r_fin, D)
            for q in (2 * KD - 2, 2 * KD - 1):
                final_square(q)
                final_scale(q)
            root(SS_FIN + 1, 4, r_fin, D)

        @block.vector
        def _(dve):
            chained = [0]

            def link(ins):
                chained[0] += 1
                ins.then_inc(dve_chain, 1)
                dve.wait_ge(dve_chain, chained[0])

            def split_low(i, src, scale, k, hf):
                dve.wait_ge(h_high, i + 1)
                o, hi = h_lo[:, k, half(hf)], h_hi[:, k, half(hf)]
                if H_ATT <= i < H_FFN:
                    o, hi = by_chunk(o), by_chunk(hi)
                if scale is None:
                    dve.tensor_tensor(o, src, hi, ALU.subtract).then_inc(h_ready, 1)
                else:
                    dve.scalar_tensor_tensor(out=o, in0=src, scalar=scale, in1=hi, op0=ALU.mult,
                                             op1=ALU.subtract).then_inc(h_ready, 1)

            def invert(n, dst):
                dve.wait_ge(rms_done, n + 1)
                link(dve.reciprocal(dst[:, half(n % 2)], dst[:, half(n % 2)]))

            def evac(g):
                n, hf, m = g // 4, (g % 4) // 2, g % 2
                dve.wait_ge(main_done, g + 1)
                if n < 2:
                    dst = yl[:, 2 * n + m, half(hf)]
                elif n < 4:
                    dst = gl[:, 2 * (n - 2) + m, half(hf)]
                elif n == 4:
                    dst = (kT, vT)[m][:, PAD + hf * HALF:PAD + (hf + 1) * HALF]
                else:
                    dst = q_tile(2 * (n - 5) + m, hf)
                src, r = main_bank(g)[0][:, :], r_mix[:, half(hf)]
                if n >= 5:
                    src, r = by_chunk(src), by_chunk(r)
                dve.tensor_tensor(dst, src, r, ALU.mult).then_inc(main_free, 1)

            def decay():
                dve.wait_ge(lam_exp, 1)
                e, z, z2, s = lam[:, 1, :], lam[:, 2, :], lam[:, 3, :], lam[:, 0, :]
                link(dve.tensor_scalar(z, e, 2.0, None, ALU.add))
                link(dve.reciprocal(z, z))
                link(dve.tensor_tensor(z, z, e, ALU.mult))
                link(dve.tensor_tensor(z2, z, z, ALU.mult))
                link(dve.tensor_scalar(s, z2, 1.0 / 15.0, None, ALU.mult))
                for d in (13.0, 11.0, 9.0, 7.0, 5.0, 3.0):
                    link(dve.scalar_tensor_tensor(out=s, in0=s, scalar=1.0 / d, in1=z2, op0=ALU.add, op1=ALU.mult))
                link(dve.scalar_tensor_tensor(out=s, in0=s, scalar=1.0, in1=z, op0=ALU.add, op1=ALU.mult))
                link(dve.tensor_scalar(e, v_lam, -1.0, 0.0, ALU.mult, ALU.max))
                link(dve.scalar_tensor_tensor(out=s, in0=s, scalar=2.0, in1=e, op0=ALU.mult, op1=ALU.add))
                dve.tensor_scalar(c_tanh, s, 4.0, None, ALU.mult).then_inc(dve_chain, 1)
                chained[0] += 1
                dve.wait_ge(dve_chain, chained[0])
                dve.tensor_scalar(c_exp, s, -8.0, None, ALU.mult).then_inc(lam_ready, 1)

            def conv(j):
                dve.wait_ge(main_free, 4 if j < 2 else 8)
                if j >= 1:
                    dve.wait_ge(state_done, j)
                link(dve.tensor_scalar(lru_x[:, :], yl[:, j, :], v_conv[:, 12 + j:13 + j], v_bconv[:, j:j + 1],
                                       ALU.mult, ALU.add))
                for s in (1, 2, 3):
                    c = 4 * (3 - s) + j
                    ins = dve.scalar_tensor_tensor(out=lru_x[:, s:], in0=yl[:, j, 0:SEQ - s],
                                                   scalar=v_conv[:, c:c + 1], in1=lru_x[:, s:],
                                                   op0=ALU.mult, op1=ALU.add)
                    if s < 3:
                        link(ins)
                    else:
                        ins.then_inc(conv_done, 1)

            def decays(j):
                dve.wait_ge(lru_exp, j + 1)
                link(dve.scalar_tensor_tensor(out=lru_u[:, :], in0=lru_r[:, :], scalar=1.0, in1=lru_u[:, :],
                                              op0=ALU.add, op1=ALU.mult))
                link(dve.tensor_scalar(lru_r[:, :], lru_u[:, :], -1.0, 1.0, ALU.mult, ALU.add))
                link(dve.scalar_tensor_tensor(out=lru_u[:, :], in0=lru_r[:, :], scalar=1.0, in1=lru_u[:, :],
                                              op0=ALU.add, op1=ALU.mult))
                dve.tensor_scalar(lru_u[:, :], lru_u[:, :], 1e-34, None, ALU.max).then_inc(lru_m2, 1)
                dve.wait_ge(conv_done, j + 1)
                link(dve.tensor_tensor(lru_x[:, :], lru_i[:, :], lru_x[:, :], ALU.mult))

            def states(j):
                dve.wait_ge(lru_root, j + 1)
                link(dve.tensor_tensor(lru_x[:, :], lru_x[:, :], lru_u[:, :], ALU.mult))
                dve.tensor_tensor_scan(yl[:, j, :], lru_r[:, :], lru_x[:, :], 0.0, ALU.mult, ALU.add
                                       ).then_inc(state_done, 1)

            dve.memset(kT[:, 0:PAD], 0.0).then_inc(pads_ready, 1)
            dve.memset(vT[:, 0:PAD], 0.0).then_inc(pads_ready, 1)
            dve.wait_ge(vec_in, 16)
            for k in range(KD):
                split_low(H_MIX + k, xT[:, k, half(0)], v_mix[:, k:k + 1], k, 0)
                add_square(dve, SS_MIX, k, sq, acc)
            dve.scalar_tensor_tensor(out=lam[:, 0, :], in0=v_lam, scalar=-1.0, in1=v_lam, op0=ALU.mult,
                                     op1=ALU.max).then_inc(lam_abs, 1)
            link(dve.tensor_scalar(nsink[:, :], sink, -1.0, None, ALU.mult))
            for k in range(KD):
                split_low(H_MIX + KD + k, xT[:, k, half(1)], v_mix[:, k:k + 1], k, 1)
                if k == 4:
                    invert(SS_MIX, r_mix)
            evac(0)
            evac(1)
            invert(SS_MIX + 1, r_mix)
            evac(2)
            evac(3)
            conv(0)
            decay()

            def multiply_y(j):
                dve.wait_ge(gelu_done, j + 1)
                dve.wait_ge(state_done, j + 1)
                dve.tensor_tensor(yl[:, j, :], yl[:, j, :], gl[:, j, :], ALU.mult).then_inc(y_done, 1)

            def norm_y(hf):
                invert(SS_LRU + hf, r_lru)
                for j in range(LT):
                    dve.wait_ge(sq_done, SQ_BY[SS_LRU + hf] - 3 + j)
                    dve.scalar_tensor_tensor(out=yl[:, j, half(hf)], in0=yl[:, j, half(hf)],
                                             scalar=v_lru[:, j:j + 1], in1=r_lru[:, half(hf)],
                                             op0=ALU.mult, op1=ALU.mult).then_inc(y_normed, 1)

            def low_y(hf):
                for j in range(LT):
                    dve.wait_ge(y_normed, 4 * hf + j + 1)
                    split_low(H_LRU + 4 * hf + j, yl[:, j, half(hf)], None, j, hf)

            def softmax_front(u):
                if u >= 2:
                    dve.wait_ge(pt_done, 2 * (u - 1))
                s = prob[:, u % 2, :]
                for g in range(NKV):
                    dve.wait_ge(s_done, 2 * u + g + 1)
                    dve.scalar_tensor_tensor(
                        out=s[:, g * 512:(g + 1) * 512].rearrange("p (c k) -> p c k", c=2),
                        in0=bank[4 + g][:, :].rearrange("p (c k) -> p c k", c=2), scalar=HD ** -0.5,
                        in1=bias[:, g * 256:(g + 1) * 256].unsqueeze(1).to_broadcast([P, 2, 256]),
                        op0=ALU.mult, op1=ALU.add).then_inc(s_read, 1)
                dve.wait_ge(s_read, 2 * u + 2)
                blocks = s.rearrange("p (b k) -> p b k", k=P)
                if u == 0:
                    for g in range(NKV):
                        link(dve.memset(s[:, g * 512:g * 512 + 256].rearrange("p (a k) -> p a k", a=2)[:, :, 0:PAD],
                                        NEG_INF))
                nm, sm = nmax[:, u % 2, :], smax[:, u % 2, :]
                link(dve.tensor_reduce(nm, blocks, AX.X, ALU.max))
                link(dve.scalar_tensor_tensor(out=nm, in0=nm, scalar=-1.0, in1=nsink[:, :], op0=ALU.mult,
                                              op1=ALU.min))
                dve.tensor_tensor(sm, sink, nm, ALU.add).then_inc(max_done, 1)

            def softmax_sum(u):
                dve.wait_ge(exp_done, 9 * (u + 1))
                d = den[:, u % 2, :]
                link(dve.tensor_tensor(d, d, esink[:, u % 2, :], ALU.add))
                dve.reciprocal(d, d).then_inc(den_done, 1)

            def read_o(u):
                dve.wait_ge(o_done, u + 1)
                dve.tensor_copy(qT[:, 2 * u:2 * u + 2, :, :],
                                bank[3][:, :].rearrange("p (c j q) -> p c j q", c=2, q=CHUNK)).then_inc(o_read, 1)

            def add_l(g):
                n, hf, m = g // 8, (g % 8) // 4, g % 4
                dve.wait_ge(main_done, L0 + g + 1)
                dst = xT[:, 4 * n + m, half(hf)]
                dve.tensor_tensor(dst, main_bank(L0 + g)[0][:, :], dst, ALU.add).then_inc(main_free, 1)

            for g in range(4, IN_GROUPS - 1):
                evac(g)
                if g - 1 in GATE_AT:
                    decays(GATE_AT.index(g - 1))
                if g - 2 in GATE_AT:
                    states(GATE_AT.index(g - 2))
                if g + 1 in GATE_AT[1:]:
                    conv(GATE_AT.index(g + 1))
                if g == 17:
                    multiply_y(0)
                    multiply_y(1)
                if g == 20:
                    multiply_y(2)
                    multiply_y(3)
                if g in (24, 25):
                    norm_y(g - 24)
            low_y(0)
            dve.wait_ge(bias_in, 16)
            dve.wait_ge(y_done, LT)
            softmax_front(0)
            evac(IN_GROUPS - 1)
            softmax_sum(0)
            softmax_front(1)
            low_y(1)
            for u in range(UNITS):
                if u >= 1:
                    read_o(u - 1)
                if u + 1 < UNITS:
                    softmax_sum(u + 1)
                add_l(2 * u)
                dve.wait_ge(pt_done, 2 * u + 2)
                if u >= 1:
                    dve.wait_ge(o_done, u)
                dve.tensor_copy(probT[:, 512:1024], bank[7][:, :]).then_inc(pt1_read, 1)
                if u + 2 < UNITS:
                    softmax_front(u + 2)
                add_l(2 * u + 1)
                if u in (5, 6):
                    for j in (2 * (u - 5), 2 * (u - 5) + 1):
                        split_low(H_ATT + j, q_tile(j, 0), v_att[:, j:j + 1], LT + j, 0)
            invert(SS_ATT, r_mix)
            read_o(UNITS - 1)
            for j in range(LT):
                split_low(H_ATT + 4 + j, q_tile(j, 1), v_att[:, j:j + 1], LT + j, 1)

            def add_a(g):
                n, hf, m = g // 8, (g % 8) // 4, g % 4
                dve.wait_ge(main_done, A0 + g + 1)
                s = scaled[:, g % 2, :]
                link(dve.tensor_tensor(s, main_bank(A0 + g)[0][:, :], r_mix[:, half(hf)], ALU.mult))
                dst = xT[:, 4 * n + m, half(hf)]
                dve.tensor_tensor(dst, dst, s, ALU.add).then_inc(main_free, 1)

            def ffn_low(k, hf):
                split_low(ffn_number(k, hf), xT[:, k, half(hf)], v_ffn[:, k:k + 1], k, hf)

            for g in range(4):
                add_a(g)
            invert(SS_ATT + 1, r_mix)
            for g in range(4, A_GROUPS):
                add_a(g)
                if g < 8:
                    ffn_low(g - 4, 0)
                elif g < 12:
                    ffn_low(g - 8, 1)
                else:
                    ffn_low(g - 8, 0)
            for k in range(4, KD):
                ffn_low(k, 1)
            invert(SS_FFN, r_ffn)

            dve.sem_inc(u_sq, RING_FREE)
            dve.sem_inc(u_ready, RING_FREE)
            dve.sem_inc(u_high, RING_FREE)

            def hidden(b, j):
                hf, m = j // 2, j % 2
                dve.wait_ge(ff1_done, 4 * b + (j + 1))
                dve.wait_ge(u_high, 4 * b + (j - 1 + RING_FREE))
                dve.wait_ge(u_sq, 4 * b + (j - 1 + RING_FREE))
                dve.scalar_tensor_tensor(out=relu[:, j % 2, :], in0=bank[j][:, :], scalar=0.0,
                                         in1=r_ffn[:, half(hf)], op0=ALU.max, op1=ALU.mult).then_inc(relu_done, 1)
                dve.wait_ge(relu_done, 4 * b + (4 + j + 1))
                dve.wait_ge(u_ready, 4 * b + (j - 1 + RING_FREE))
                dve.tensor_tensor(usq[:, j % 2, :], relu[:, j % 2, :], relu[:, j % 2, :], ALU.mult
                                  ).then_inc(u_sq, 1)
                dve.wait_ge(u_sq, 4 * b + (RING_FREE + j + 1))
                dve.wait_ge(u_high, 4 * b + (RING_FREE + j + 1))
                dve.tensor_tensor(u_lo[:, m, half(hf)], usq[:, j % 2, :], u_hi[:, m, half(hf)],
                                  ALU.subtract).then_inc(u_ready, 1)

            def add_ff(b, q):
                hf, m = q // KD, q % KD
                dve.wait_ge(ff2_done, 16 * b + (q + 1))
                dst = xT[:, m, half(hf)]
                dve.tensor_tensor(dst, bank[4 + q % 4][:, :], dst, ALU.add).then_inc(y_added, 1)

            for j in range(4):
                if j == 2:
                    invert(SS_FFN + 1, r_ffn)
                hidden(0, j)
            for q in range(16):
                add_ff(0, q)
                if q >= 12:
                    i = q - 12
                    k, hf = i % 2, i // 2
                    dve.wait_ge(pp_high, i + 1)
                    dve.tensor_tensor(pT_lo[:, k, half(hf)], pT[:, k, half(hf)], pT_hi[:, k, half(hf)],
                                      ALU.subtract).then_inc(pp_ready, 1)
            with dve.Fori(1, FF_BLOCKS - 1) as b:
                for j in range(4):
                    hidden(b, j)
                for q in range(16):
                    add_ff(b, q)
            for j in range(4):
                hidden(FF_BLOCKS - 1, j)
            for q in range(16):
                add_ff(FF_BLOCKS - 1, q)
                if q >= KD:
                    k = q - KD
                    split_low(H_PLE + k, xT[:, k, half(0)], v_ple[:, k:k + 1], k, 0)
            for k in range(4):
                split_low(H_PLE + KD + k, xT[:, k, half(1)], v_ple[:, k:k + 1], k, 1)
            invert(SS_PLE, r_mix)

            def gate_scale(q):
                hf, m = q // KD, q % KD
                dve.wait_ge(gate_done, q + 1)
                if q >= 2:
                    dve.wait_ge(x_gated, 2 * (q - 1))
                dve.tensor_tensor(gt[:, q % 2, :], bank[q % 2][:, :], r_mix[:, half(hf)], ALU.mult
                                  ).then_inc(gate_scaled, 1)

            def gate_add(q):
                hf, m = q // KD, q % KD
                dve.wait_ge(gate_sig, q + 1)
                dve.wait_ge(ple_done, q + 1)
                dve.tensor_tensor(gt[:, q % 2, :], bank[2 + q % 2][:, :], gt[:, q % 2, :], ALU.mult
                                  ).then_inc(x_gated, 1)
                dve.wait_ge(x_gated, 2 * q + 1)
                dve.tensor_tensor(xT[:, m, half(hf)], xT[:, m, half(hf)], gt[:, q % 2, :], ALU.add
                                  ).then_inc(x_gated, 1)

            def out_tile(k):
                dve.scalar_tensor_tensor(out=o_ring[:, k, :], in0=xT[:, k, half(0)], scalar=v_fin[:, k:k + 1],
                                         in1=r_fin[:, half(0)], op0=ALU.mult, op1=ALU.mult
                                         ).then_inc(out_ready[k], 1)

            for q in range(2 * KD):
                gate_scale(q)
                if q == 0:
                    for k in range(4, KD):
                        split_low(H_PLE + KD + k, xT[:, k, half(1)], v_ple[:, k:k + 1], k, 1)
                if q == 5:
                    invert(SS_PLE + 1, r_mix)
                if q % 2 == 1:
                    gate_add(q - 1)
                    gate_add(q)
                if q == KD + 4:
                    invert(SS_FIN, r_fin)
                if q >= KD + 4:
                    out_tile(2 * (q - KD - 4))
                    out_tile(2 * (q - KD - 4) + 1)
            dve.wait_ge(rms_done, SS_FIN + 2)
            dve.reciprocal(r_fin[:, half(1)], r_fin[:, half(1)]).then_inc(fin_ready, 1)
            dve.wait_ge(fin_ready, 1)
            dve.wait_ge(x_scaled, KD)
            for k in DVE_OUT:
                dve.wait_ge(out_done[k], 16)
                dve.tensor_tensor(o_ring[:, k, :], xT[:, k, half(1)], r_fin[:, half(1)], ALU.mult
                                  ).then_inc(out_ready[k], 1)


def kernel(**inputs):
    import concourse.bacc as bacc
    from concourse.bass_utils import run_bass_kernel_spmd

    f = {n: np.asarray(a) for n, a in inputs.items()}

    def pieces(w, kt):
        rows, cols = w.shape
        c = PIECE // kt
        w = w.reshape(rows // (kt * P), 2, kt // 2, P, cols // c, c)
        return np.ascontiguousarray(w.transpose(0, 4, 1, 3, 2, 5).reshape(-1, 2, P, HP))

    heads = np.arange(ATT).reshape(NKV, NQ // NKV, HD).transpose(1, 0, 2).ravel()
    w_in = f["w_in"][0]
    o2, o3 = 2 * LRU, 2 * LRU + ATT
    w_in = np.concatenate([w_in[:, :o2], w_in[:, o3:], w_in[:, o2:o3][:, heads]], axis=1)
    w_out = np.concatenate([f["w_out"][0][:LRU], f["w_out"][0][LRU:][heads]], axis=0)
    gates_w = np.zeros((P, 2, LT, P), np.float32)
    for i, n in enumerate(("w_lru_a", "w_lru_i")):
        for j in range(LT):
            for b in range(2):
                gates_w[b * HD:(b + 1) * HD, i, j, b * HD:(b + 1) * HD] = f[n][0, 2 * j + b]
    sinks = f["sinks"][0].reshape(NKV, 1, 2, 2).repeat(2, axis=1).transpose(3, 0, 1, 2).reshape(2, 1, 8).repeat(
        HD, axis=1).reshape(P, 8)
    columns = {n: f[n].reshape(-1, P).T for n in VEC if n != "sinks"}
    columns["g_attn_out"] = f["g_attn_out"][0][heads].reshape(-1, P).T
    columns["sinks"] = sinks
    arrays = {
        "x": np.ascontiguousarray(f["x"][0].T),
        "p": np.ascontiguousarray(f["p"][0, 0].T),
        "vectors": np.ascontiguousarray(np.concatenate([columns[n] for n in VEC], axis=1)),
        "gates_w": gates_w,
        "w_in": pieces(w_in, KD),
        "w_out": pieces(w_out, LT),
        "w_ff1": pieces(f["w_ff1"][0], KD),
        "w_ff2": pieces(f["w_ff2"][0], 2),
        "w_ple_gate": pieces(f["w_ple_gate"][0], KD),
        "w_ple_proj": pieces(f["w_ple_proj"][0], 2),
    }
    head = (4 * np.arange(2)[None, :, None] + 2 * np.arange(2)[None, None, :]
            + np.repeat(np.arange(2), HD)[:, None, None])
    dist = np.abs(CHUNK + np.tile(np.arange(CHUNK), 2)[:, None] - np.arange(2 * CHUNK)[None, :])
    arrays["alibi"] = (-(2.0 ** -(head + 1.0))[:, :, :, None] * dist[:, None, None, :]).reshape(P, 512).astype(
        np.float32)
    nc = bacc.Bacc("TRN2", target_bir_lowering=False, num_devices=1, dynamic_dma_scratch_size=1024)
    args = {n: nc.dram_tensor(f"in_{n}", a.shape, mybir.dt.from_np(a.dtype), kind="ExternalInput").ap()
            for n, a in arrays.items()}
    out = nc.dram_tensor("out_x", (D, SEQ), F32, kind="ExternalOutput").ap()
    build(nc, out=out, **args)
    r = run_bass_kernel_spmd(nc, [{f"in_{n}": a for n, a in arrays.items()}], core_ids=[0])
    return np.ascontiguousarray(r.results[0]["out_x"].T).reshape(1, SEQ, D)
```

```python
from contextlib import ExitStack

import numpy as np

import concourse.bass as bass
from concourse import mybir

F32 = mybir.dt.float32
F32R = mybir.dt.float32r
ALU = mybir.AluOpType
ACT = mybir.ActivationFunctionType
AX = mybir.AxisListType

P = 128
SEQ = 1024
D = 1024
KD = D // P
HALF = SEQ // 2
LRU = D // 2
LT = LRU // P
ATT = D // 2
HD = 64
NQ, NKV = 8, 2
CHUNK = 64
KVW = NKV * HD
IN_W = 2 * LRU + ATT + 2 * KVW
FF = 4 * D
PLE = 256
EPS = 1e-6
NEG_INF = -1e30
UNITS = SEQ // (2 * CHUNK)
PAD = CHUNK

PIECE = 2048
HP = PIECE // 2
QP = HP // 2
STAGES = 4
IN_PIECES = IN_W // 256
OUT_PIECES = 4
FF_BLOCK = 256
FF_BLOCKS = FF // FF_BLOCK
GATE_PIECES = D // 256
PARTS = ((0, HALF), (HALF, HALF // 2), (HALF + HALF // 2, HALF // 2))
LAST = len(PARTS) - 1
FF_FIRST = IN_PIECES + OUT_PIECES
GATE_FIRST = FF_FIRST + 2 * FF_BLOCKS

IN_GROUPS = 4 * IN_PIECES
L_GROUPS = 16
A_GROUPS = 16
L0 = IN_GROUPS
A0 = L0 + L_GROUPS
MAIN_GROUPS = A0 + A_GROUPS
IN_BANKS = 4
OUT_BANKS = 3
A_BANKS = (1, 2, 0, 3)
GATE_AT = [5, 9, 13, 17]

H_MIX, H_LRU, H_ATT, H_FFN, H_PLE = 0, 16, 24, 32, 48
SS_MIX, SS_LRU, SS_ATT, SS_FFN, SS_PLE, SS_FIN = 0, 2, 4, 6, 8, 10
SQ_TILES = [8, 8, 4, 4, 4, 4, 8, 8, 8, 8] + [KD] * len(PARTS)
SQ_BY = [sum(SQ_TILES[:n + 1]) for n in range(len(SQ_TILES))]
RING = 2
POOL_OUT, DVE_OUT = (6, 7), (0, 1, 2, 3, 4, 5)
OUT_AT = {14: ((0, 0), (1, 0)), 15: ((2, 0), (3, 0)), 16: ((4, 0),), 17: ((5, 0),), 18: ((6, 0),), 19: ((7, 0),),
          21: ((0, 1), (1, 1)), 22: ((2, 1),), 23: ((3, 1), (4, 1), (5, 1), (6, 1), (7, 1))}
LAST_STORES = (slice(0, 1), slice(1, 3), slice(6, 8), slice(3, 5), slice(5, 6))
RING_FREE = 2


VEC = {}
for _name, _n in (("g_mix", KD), ("w_conv", 4 * LT), ("b_conv", LT), ("b_lru_a", LT), ("b_lru_i", LT),
                  ("lru_lambda", LT), ("g_lru_out", LT), ("g_attn_out", LT), ("g_ffn", KD), ("g_ple", KD),
                  ("g_final", KD), ("sinks", 8)):
    VEC[_name] = slice(sum(v.stop - v.start for v in VEC.values()), sum(v.stop - v.start for v in VEC.values()) + _n)
NVEC = sum(v.stop - v.start for v in VEC.values())


def build(nc, x, p, vectors, gates_w, w_in, w_out, w_ff1, w_ff2, w_ple_gate, w_ple_proj, alibi, out):
    ctx = ExitStack()
    with ctx:
        KB = 1024
        base = -(-(nc.sbuf_base) // 32) * 32

        def at(name, offset, shape, dt=F32):
            return nc.alloc_sbuf_tensor_at(name, shape, dt, offset=base + offset)

        def sem(name):
            return ctx.enter_context(nc.semaphore(name))

        XT, HH, HL, WH, WL, ST = 0, 32 * KB, 64 * KB, 96 * KB, 112 * KB, 128 * KB
        T, Y, G, Q = 144 * KB, 160 * KB, 176 * KB, 192 * KB
        KV = 208 * KB
        xT = at("xT", XT, [P, KD, SEQ])
        h_hi = at("h_hi", HH, [P, KD, SEQ], F32R)
        h_lo = at("h_lo", HL, [P, KD, SEQ], F32R)
        w_hi = at("w_hi", WH, [P, 2, PIECE], F32R)
        w_lo = at("w_lo", WL, [P, 2, PIECE], F32R)
        stage = at("stage", ST, [P, STAGES, HP])
        gate_w = at("gate_w", KV + 4 * PAD, [P, 2, LT, P])
        gw_hi = at("gw_hi", Q, [P, 2, LT, P], F32R)
        gw_lo = at("gw_lo", Q + 4 * KB, [P, 2, LT, P], F32R)
        gx_hi = at("gx_hi", Q + 8 * KB, [P, SEQ], F32R)
        gx_lo = at("gx_lo", Q + 12 * KB, [P, SEQ], F32R)
        sq = at("sq", T, [P, RING, HALF])
        acc = at("acc", T + 4 * KB, [P, SEQ])
        lru_r = at("lru_r", T, [P, SEQ])
        lru_i = at("lru_i", T + 4 * KB, [P, SEQ])
        lru_u = at("lru_u", T + 8 * KB, [P, SEQ])
        lru_x = at("lru_x", T + 12 * KB, [P, SEQ])
        yl = at("yl", Y, [P, LT, SEQ])
        gl = at("gl", G, [P, LT, SEQ])
        r_lru = at("r_lru", G + 12 * KB, [P, SEQ])
        qT = at("qT", Q, [P, SEQ // CHUNK, LT, CHUNK])
        kT = at("kT", KV, [P, PAD + SEQ])
        vT = at("vT", KV + 4 * (PAD + SEQ), [P, PAD + SEQ])
        v_win = at("v_win", T + 8 * KB, [P, SEQ // CHUNK, P])
        prob = at("prob", G, [P, 2, 1024])
        probT = at("probT", G + 8 * KB, [P, 1024])
        bias = at("bias", G + 12 * KB, [P, 512])
        scaled = at("scaled", T + 8 * KB, [P, 2, HALF])
        r_ffn = at("r_ffn", KV, [P, SEQ])
        u_hi = at("u_hi", Y, [P, 2, SEQ], F32R)
        u_lo = at("u_lo", Y + 8 * KB, [P, 2, SEQ], F32R)
        relu = at("relu", G, [P, 2, HALF])
        usq = at("usq", G + 4 * KB, [P, 2, HALF])
        pT = at("pT", G + 8 * KB, [P, 2, SEQ])
        pT_hi = at("pT_hi", T, [P, 2, SEQ], F32R)
        pT_lo = at("pT_lo", T + 8 * KB, [P, 2, SEQ], F32R)
        pw_hi = at("pw_hi", Q, [P, PIECE], F32R)
        pw_lo = at("pw_lo", Q + 8 * KB, [P, PIECE], F32R)
        gt = at("gt", G, [P, 2, HALF])
        r_fin = at("r_fin", KV, [P, SEQ])
        sq2 = at("sq2", G + 4 * KB, [P, RING, HALF])
        acc2 = at("acc2", KV + 4 * (PAD + SEQ), [P, SEQ])
        o_ring = at("o_ring", Y, [P, KD, HALF])
        at_byte = KV + 2 * 4 * (PAD + SEQ)
        small = {}
        for name, shape in (("r_mix", [P, SEQ]), ("ident", [P, P]), ("ones", [P, P]), ("vec", [P, NVEC]),
                            ("nsink", [P, 8]), ("eps", [P, 1]),
                            ("lam", [P, 6, LT]), ("nmax", [P, 2, 8]), ("smax", [P, 2, 8]),
                            ("esink", [P, 2, 8]), ("den", [P, 2, 8])):
            small[name] = at(name, at_byte, shape)
            at_byte += -(-4 * int(np.prod(shape[1:])) // 32) * 32
        r_mix, ident, ones, vec = (small[n] for n in ("r_mix", "ident", "ones", "vec"))
        nsink, eps, lam = (small[n] for n in ("nsink", "eps", "lam"))
        nmax, smax, esink, den = (small[n] for n in ("nmax", "smax", "esink", "den"))
        (v_mix, v_conv, v_bconv, v_ba, v_bi, v_lam, v_lru, v_att, v_ffn, v_ple, v_fin, sink) = (
            vec[:, VEC[n]] for n in VEC)
        c_tanh, c_exp = lam[:, 4, :], lam[:, 5, :]

        bank = [ctx.enter_context(nc.psum_tensor(f"bank{i}", [P, HALF], F32)) for i in range(8)]

        x_in = [sem(f"x_in{i}") for i in range(8)]
        stage_in = [sem(f"stage_in{i}") for i in range(STAGES)]
        gw_high, gw_split, gx_high, gx_low = (sem(n) for n in ("gw_high", "gw_split", "gx_high", "gx_low"))
        vec_in, gatew_in, bias_in, p_in = sem("vec_in"), sem("gatew_in"), sem("bias_in"), sem("p_in")
        first_w_in, first_x_in, last_done = sem("first_w_in"), sem("first_x_in"), sem("last_done")
        first_high, first_low = sem("first_high"), sem("first_low")
        out_ready = [sem(f"out_ready{k}") for k in range(KD)]
        out_done = [sem(f"out_done{pair}") for pair in range(KD // 2)]
        consts, w_split, sq_used, p_ready, pool_chain = (
            sem(n) for n in ("consts", "w_split", "sq_used", "p_ready", "pool_chain"))
        main_done, gates_done, ss_done, vt_done, s_done, pt_done, o_done, ff1_done, ff2_done, gate_done, ple_done = (
            sem(n) for n in ("main_done", "gates_done", "ss_done", "vt_done", "s_done", "pt_done", "o_done",
                             "ff1_done", "ff2_done", "gate_done", "ple_done"))
        w_high, h_high, sq_done, rms_done, lam_exp, gates_sig, lru_tanh, lru_exp, lru_root = (
            sem(n) for n in ("w_high", "h_high", "sq_done", "rms_done", "lam_exp", "gates_sig", "lru_tanh",
                             "lru_exp", "lru_root"))
        gelu_done, vt_read, exp_done, pt0_read, u_high, pp_high, gate_sig, x_scaled = (
            sem(n) for n in ("gelu_done", "vt_read", "exp_done", "pt0_read", "u_high", "pp_high", "gate_sig",
                             "x_scaled"))
        dve_chain, lam_abs, lam_ready, h_ready, main_free, conv_done, lru_m2, state_done = (
            sem(n) for n in ("dve_chain", "lam_abs", "lam_ready", "h_ready", "main_free", "conv_done", "lru_m2",
                             "state_done"))
        y_done, y_normed, s_read, max_done, den_done, pt1_read, o_read, pads_ready = (
            sem(n) for n in ("y_done", "y_normed", "s_read", "max_done", "den_done", "pt1_read", "o_read",
                             "pads_ready"))
        relu_done, u_sq, u_ready, y_added, pp_ready, gate_scaled, x_gated, fin_ready = (
            sem(n) for n in ("relu_done", "u_sq", "u_ready", "y_added", "pp_ready", "gate_scaled", "x_gated",
                             "fin_ready"))

        def half(hf):
            return slice(hf * HALF, (hf + 1) * HALF)

        def ffn_number(k, hf):
            return H_FFN + 8 * (k // 4) + 4 * hf + k % 4

        def q_tile(j, hf):
            return qT[:, hf * 8:(hf + 1) * 8, j, :]

        def by_chunk(ap):
            return ap.rearrange("p (c q) -> p c q", q=CHUNK)

        def slot(n):
            return (n - (n > GATE_FIRST)) % 2

        def main_bank(g):
            if g < L0:
                return bank[g % IN_BANKS], g - IN_BANKS if g >= IN_BANKS else None
            if g < A0:
                i = (g - L0) % OUT_BANKS
                if g - L0 < OUT_BANKS:
                    return bank[i], max(q for q in range(L0) if q % IN_BANKS == i)
                return bank[i], g - OUT_BANKS
            i = A_BANKS[(g - A0) % 4]
            if g - A0 < 4:
                return bank[i], max(q for q in range(L0, A0) if (q - L0) % OUT_BANKS == i) if i < OUT_BANKS else None
            return bank[i], g - 4

        def piece_free(eng, n):
            if n < IN_PIECES:
                eng.wait_ge(main_done, 4 * (n + 1))
            else:
                eng.wait_ge(main_done, IN_GROUPS + 8 * (n - IN_PIECES + 1))

        def tokens(part):
            return slice(PARTS[part][0], sum(PARTS[part]))

        def span(n):
            return (half(n % 2), HALF) if n < SS_FIN else (tokens(n - SS_FIN), PARTS[n - SS_FIN][1])

        def ring_tile(ring, q):
            return ring[:, q % RING, :] if q < SQ_BY[SS_FIN] else ring[:, q % RING, 0:PARTS[LAST][1]]

        def result(k, part):
            first, width = PARTS[part]
            return o_ring[:, k, first % HALF:first % HALF + width]

        def add_square(eng, n, i, ring, total):
            q = SQ_BY[n] - SQ_TILES[n] + i
            if n >= 2 and i == 0:
                eng.wait_ge(ss_done, n - 1)
            eng.wait_ge(sq_done, q + 1)
            if q >= 1:
                eng.wait_ge(sq_used, q)
            dst, src = total[:, span(n)[0]], ring_tile(ring, q)
            if i == 0:
                eng.tensor_copy(dst, src).then_inc(sq_used, 1)
            else:
                eng.tensor_tensor(dst, dst, src, ALU.add).then_inc(sq_used, 1)

        block = ctx.enter_context(nc.Block())

        @block.sync
        def _(sp):
            def load_x(i):
                hf, k = i // 4, 2 * (i % 4)
                sp.dma_start(xT[:, k:k + 2, half(hf)], x.rearrange("(k p) t -> p k t", p=P)[:, k:k + 2, half(hf)]
                             ).then_inc(x_in[i], 16)

            def load_half(s, src):
                if s >= STAGES:
                    sp.wait_ge(w_split, s - STAGES + 1)
                sp.dma_start(stage[:, s % STAGES, :], src).then_inc(stage_in[s % STAGES], 16)

            def load_piece(n, w, i):
                for h in range(2):
                    load_half(2 * n + h, w[i, h])

            sp.dma_start(stage[:, 0, 0:QP], w_in[0, 0, :, 0:QP]).then_inc(first_w_in, 16)
            sp.dma_start(vec[:, :], vectors).then_inc(vec_in, 16)
            sp.dma_start(xT[:, 0, half(0)], x[0:P, half(0)]).then_inc(first_x_in, 16)
            sp.dma_start(stage[:, 0, QP:HP], w_in[0, 0, :, QP:HP]).then_inc(stage_in[0], 16)
            sp.dma_start(xT[:, 1, half(0)], x[P:2 * P, half(0)]).then_inc(x_in[0], 16)
            load_x(1)
            load_half(1, w_in[0, 1])
            load_x(2)
            for i in range(3, 8):
                load_x(i)
            for n in range(1, IN_PIECES):
                load_piece(n, w_in, n)
                if n == 1:
                    sp.dma_start(gate_w[:, :, :, :], gates_w).then_inc(gatew_in, 16)
            load_piece(IN_PIECES, w_out, 0)
            sp.wait_ge(y_normed, LT)
            sp.dma_start(bias[:, :], alibi).then_inc(bias_in, 16)
            for i in range(1, OUT_PIECES):
                load_piece(IN_PIECES + i, w_out, i)
            with sp.Fori(0, FF_BLOCKS) as b:
                for i in range(4):
                    s0 = 2 * FF_FIRST + i
                    sp.wait_ge(w_split, 4 * b + (s0 - STAGES + 1))
                    sp.dma_start(stage[:, s0 % STAGES, :], (w_ff1 if i < 2 else w_ff2)[b, i % 2]
                                 ).then_inc(stage_in[s0 % STAGES], 16)
            for i in range(1 + GATE_PIECES * len(PARTS)):
                if i == 1:
                    load_piece(GATE_FIRST + i, w_ple_proj, 0)
                else:
                    load_piece(GATE_FIRST + i, w_ple_gate, (0 if i == 0 else i - 1) % GATE_PIECES)
            out_tiles = out.rearrange("(k p) t -> p k t", p=P)
            for part in range(LAST):
                for pair in range(KD // 2):
                    k = 2 * pair
                    sp.wait_ge(out_ready[k], part + 1)
                    sp.wait_ge(out_ready[k + 1], part + 1)
                    sp.dma_start(out_tiles[:, k:k + 2, tokens(part)], result(slice(k, k + 2), part)
                                 ).then_inc(out_done[pair], 16)
            for run in LAST_STORES:
                for k in range(run.start, run.stop):
                    sp.wait_ge(out_ready[k], LAST + 1)
                sp.dma_start(out_tiles[:, run, tokens(LAST)], result(run, LAST)).then_inc(last_done, 16)
            for pair in range(KD // 2):
                sp.wait_ge(out_done[pair], 16 * LAST)
            sp.wait_ge(last_done, 16 * len(LAST_STORES))

        @block.gpsimd
        def _(pool):
            pool.memset(ident[:, :], 0.0).then_inc(pool_chain, 1)
            pool.memset(ones[:, :], 1.0).then_inc(consts, 1)
            pool.memset(eps[:, :], EPS).then_inc(consts, 1)
            pool.wait_ge(pool_chain, 1)
            pool.affine_select(out=ident[:, :], in_=ident[:, :], compare_op=ALU.not_equal, fill=1.0,
                               base=0, pattern=[[-1, P]], channel_multiplier=1).then_inc(consts, 1)

            def low(s, dst=None):
                n = s // 2
                pool.wait_ge(w_high, s + 1)
                o = (s % 2) * HP
                lo, hi = (w_lo[:, slot(n), o:o + HP], w_hi[:, slot(n), o:o + HP]) if dst is None else dst
                pool.tensor_tensor(lo, stage[:, s % STAGES, :], hi, ALU.subtract).then_inc(w_split, 1)

            def sums(n, ring, total):
                for i in range(SQ_TILES[n]):
                    add_square(pool, n, i, ring, total)

            def probs(u):
                pool.wait_ge(den_done, u + 1)
                e = prob[:, u % 2, :].rearrange("p (b k) -> p b k", k=P)
                pool.tensor_tensor(e, e, den[:, u % 2, :].unsqueeze(2).to_broadcast([P, 8, P]),
                                   ALU.mult).then_inc(p_ready, 1)

            pool.wait_ge(w_split, 1)
            low(1)
            for i in range(2, KD):
                add_square(pool, SS_MIX + 1, i, sq, acc)
            low(2)
            low(3)
            pool.wait_ge(gw_high, 1)
            pool.tensor_tensor(gw_lo[:, :, :, :], gate_w[:, :, :, :], gw_hi[:, :, :, :], ALU.subtract
                               ).then_inc(gw_split, 1)

            def gate_input_low(j):
                if j >= 1:
                    pool.wait_ge(gates_done, 4 * j)
                for hf in range(2):
                    pool.wait_ge(gx_high, 2 * j + hf + 1)
                    pool.tensor_tensor(gx_lo[:, half(hf)], lru_x[:, half(hf)], gx_hi[:, half(hf)], ALU.subtract
                                       ).then_inc(gx_low, 1)

            for n in range(2, IN_PIECES):
                low(2 * n)
                low(2 * n + 1)
                if n - 2 < LT:
                    gate_input_low(n - 2)
                if n == 5:
                    sums(SS_LRU, sq, acc)
                    sums(SS_LRU + 1, sq, acc)
            low(2 * 7)
            low(2 * 7 + 1)
            probs(0)
            probs(1)
            low(2 * 8)
            low(2 * 8 + 1)
            for u in range(2, UNITS):
                if u == 6:
                    low(2 * 9)
                    low(2 * 9 + 1)
                probs(u)
            low(2 * 10)
            low(2 * 10 + 1)
            sums(SS_FFN, sq, acc)
            low(2 * FF_FIRST)
            low(2 * FF_FIRST + 1)
            sums(SS_FFN + 1, sq, acc)
            with pool.Fori(0, FF_BLOCKS) as b:
                for i in range(4):
                    s0 = 2 * FF_FIRST + 2 + i
                    n0, o = s0 // 2, (s0 % 2) * HP
                    pool.wait_ge(w_high, 4 * b + (s0 + 1))
                    pool.tensor_tensor(w_lo[:, n0 % 2, o:o + HP], stage[:, s0 % STAGES, :],
                                       w_hi[:, n0 % 2, o:o + HP], ALU.subtract).then_inc(w_split, 1)
            sums(SS_PLE, sq2, acc2)
            s0 = 2 * (GATE_FIRST + 1)
            for s in (s0, s0 + 1):
                o = (s % 2) * HP
                low(s, (pw_lo[:, o:o + HP], pw_hi[:, o:o + HP]))
            low(s0 + 2)
            low(s0 + 3)
            sums(SS_PLE + 1, sq2, acc2)
            for q in range(len(PARTS) * KD):
                if q >= 2:
                    add_square(pool, SS_FIN + (q - 2) // KD, (q - 2) % KD, sq2, acc2)
                if q % 2 == 1 and q // 2 + 2 < GATE_PIECES * len(PARTS):
                    low(2 * (GATE_FIRST + 3 + q // 2))
                    low(2 * (GATE_FIRST + 3 + q // 2) + 1)
            add_square(pool, SS_FIN + LAST, KD - 2, sq2, acc2)
            pool.wait_ge(x_scaled, KD)
            pool.wait_ge(fin_ready, 1)
            for k in POOL_OUT:
                pool.wait_ge(out_done[k // 2], 16)
                pool.tensor_tensor(result(k, LAST), xT[:, k, tokens(LAST)], r_fin[:, tokens(LAST)], ALU.mult
                                   ).then_inc(out_ready[k], 1)

        @block.tensor
        def _(pe):
            def passes(o, whi, wlo, hh, hl, first, last):
                pe.matmul(o, whi, hh, start=first, stop=False)
                pe.matmul(o, whi, hl, start=False, stop=False)
                return pe.matmul(o, wlo, hh, start=False, stop=last)

            def group(g, n, kt, m, hf, k_h, h_first, ready, middle=None):
                cols = PIECE // kt
                o, before = main_bank(g)
                o = o[:, :]
                if before is not None:
                    pe.wait_ge(main_free, before + 1)
                for k in range(kt):
                    if ready and k == 0:
                        pe.wait_ge(w_split, 2 * n + 1)
                    if ready and k == kt // 2:
                        pe.wait_ge(w_split, 2 * n + 2)
                    if h_first is not None:
                        pe.wait_ge(h_ready, h_first + k + 1)
                    if middle is not None and k == kt // 2:
                        middle()
                    c = k * cols + m * P
                    sl = [w[:, n % 2, c:c + P] for w in (w_hi, w_lo)]
                    hh, hl = h_hi[:, k_h + k, half(hf)], h_lo[:, k_h + k, half(hf)]
                    last = passes(o, sl[0], sl[1], hh, hl, k == 0, k == kt - 1)
                last.then_inc(main_done, 1)

            def first_groups(hf):
                g = 2 * hf
                for k in range(KD):
                    if hf == 0 and k == 0:
                        pe.wait_ge(first_low, 1)
                    if hf == 0 and k in (2, 4):
                        pe.wait_ge(w_split, k // 2)
                    pe.wait_ge(h_ready, H_MIX + 8 * hf + k + 1)
                    for m in range(2):
                        c = k * 256 + m * P
                        last = passes(bank[g + m][:, :], w_hi[:, 0, c:c + P], w_lo[:, 0, c:c + P],
                                      h_hi[:, k, half(hf)], h_lo[:, k, half(hf)], k == 0, k == KD - 1)
                        if k == KD - 1:
                            last.then_inc(main_done, 1)

            def sum_rows(n, total, b):
                pe.wait_ge(sq_used, SQ_BY[n])
                if n >= 1:
                    pe.wait_ge(rms_done, n)
                tok, width = span(n)
                pe.matmul(bank[b][:, 0:width], ones[:, :], total[:, tok], start=True, stop=True
                          ).then_inc(ss_done, 1)

            def gates(j):
                pe.wait_ge(gw_split, 1)
                for hf in range(2):
                    pe.wait_ge(gx_low, 2 * j + hf + 1)
                    for i in range(2):
                        b = 4 + 2 * hf + i
                        if j >= 1:
                            pe.wait_ge(gates_sig, 4 * (j - 1) + 2 * hf + i + 1)
                        else:
                            pe.wait_ge(rms_done, SS_MIX + 2)
                        passes(bank[b][:, :], gw_hi[:, i, j, :], gw_lo[:, i, j, :], gx_hi[:, half(hf)],
                               gx_lo[:, half(hf)], True, True).then_inc(gates_done, 1)

            def turn_v(i):
                pe.wait_ge(main_free, 4 * 4 + 4)
                pe.wait_ge(pads_ready, 2)
                if i >= 2:
                    pe.wait_ge(vt_read, i - 1)
                else:
                    pe.wait_ge(gates_sig, 16)
                for c in range(4 * i, 4 * i + 4):
                    last = pe.transpose(bank[6 + i % 2][:, (c % 4) * P:(c % 4 + 1) * P],
                                        vT[:, c * CHUNK:c * CHUNK + P], ident[:, :])
                last.then_inc(vt_done, 1)

            def scores(u):
                pe.wait_ge(main_free, IN_GROUPS - (0 if u >= UNITS // 2 else 2))
                for g in range(NKV):
                    if u >= 1:
                        pe.wait_ge(s_read, 2 * (u - 1) + g + 1)
                    else:
                        pe.wait_ge(rms_done, SS_LRU + 2)
                    r = slice(g * HD, (g + 1) * HD)
                    for cp in range(2):
                        c = 2 * u + cp
                        for a in range(2):
                            last = pe.matmul(bank[4 + g][:, (2 * cp + a) * P:(2 * cp + a + 1) * P],
                                             qT[r, c, 2 * a:2 * a + 2, :].rearrange("p a q -> p (a q)"),
                                             kT[r, c * CHUNK:c * CHUNK + P], start=True, stop=True)
                    last.then_inc(s_done, 1)

            def turn_p(u):
                pe.wait_ge(p_ready, u + 1)
                for g in range(NKV):
                    if u >= 1:
                        pe.wait_ge(pt0_read if g == 0 else pt1_read, u)
                    else:
                        pe.wait_ge(vt_read, 4)
                    for i in range(4):
                        last = pe.transpose(bank[6 + g][:, i * P:(i + 1) * P],
                                            prob[:, u % 2, (4 * g + i) * P:(4 * g + i + 1) * P], ident[:, :])
                    last.then_inc(pt_done, 1)

            def values(u):
                pe.wait_ge(pt0_read, u + 1)
                pe.wait_ge(pt1_read, u + 1)
                if u >= 1:
                    pe.wait_ge(o_read, u)
                else:
                    pe.wait_ge(main_free, L0)
                for cp in range(2):
                    for g in range(NKV):
                        last = pe.matmul(bank[3][g * HD:(g + 1) * HD, cp * 256:(cp + 1) * 256],
                                         v_win[:, 2 * u + cp, g * HD:(g + 1) * HD],
                                         probT[:, g * 512 + cp * 256:g * 512 + (cp + 1) * 256],
                                         start=True, stop=True)
                last.then_inc(o_done, 1)

            pe.wait_ge(consts, 3)
            first_groups(0)
            sum_rows(SS_MIX, acc, 7)
            first_groups(1)
            sum_rows(SS_MIX + 1, acc, 7)
            for g in range(4, IN_GROUPS):
                n, hf, m = g // 4, (g % 4) // 2, g % 2
                middle = None
                if g - 1 in GATE_AT:
                    middle = lambda: gates(GATE_AT.index(g - 1))
                if g >= 26:
                    middle = lambda: scores(g - 26)
                group(g, n, KD, m, hf, 0, None, g % 4 == 0, middle)
                if g in (22, 23):
                    sum_rows(SS_LRU + g - 22, acc, 5)
                if 21 <= g < 25:
                    turn_v(g - 21)
            for u in range(UNITS):
                for i in range(2):
                    g = 2 * u + i
                    n, hf, m = g // 8, (g % 8) // 4, g % 4
                    group(L0 + g, IN_PIECES + n, LT, m, hf, 0, H_LRU + 4 * hf if n == 0 and m == 0 else None,
                          g % 8 == 0)
                    if i == 0:
                        turn_p(u)
                        if u + 2 < UNITS:
                            scores(u + 2)
                if u == UNITS - 1:
                    pe.wait_ge(s_read, 2 * UNITS)
                    sum_rows(SS_ATT, acc, 4)
                values(u)
            for g in range(A_GROUPS):
                n, hf, m = g // 8, (g % 8) // 4, g % 4
                if g == 3:
                    pe.wait_ge(o_read, UNITS)
                group(A0 + g, IN_PIECES + 2 + n, LT, m, hf, LT, H_ATT + 4 * hf if n == 0 and m == 0 else None,
                      g % 8 == 0)
                if g == 4:
                    sum_rows(SS_ATT + 1, acc, 5)
                if g == 14:
                    sum_rows(SS_FFN, acc, 7)

            n1, n2 = FF_FIRST % 2, (FF_FIRST + 1) % 2

            def ff1(b, hf, m):
                j = 2 * hf + m
                if j == 0:
                    pe.wait_ge(w_split, 4 * b + 2 * (FF_FIRST + 1))
                pe.wait_ge(relu_done, 4 * b + (j + 1))
                for k in range(KD):
                    c = k * 256 + m * P
                    hh, hl = h_hi[:, k, half(hf)], h_lo[:, k, half(hf)]
                    last = passes(bank[j][:, :], w_hi[:, n1, c:c + P], w_lo[:, n1, c:c + P], hh, hl,
                                  k == 0, k == KD - 1)
                last.then_inc(ff1_done, 1)

            def ff2(b):
                pe.wait_ge(w_split, 4 * b + 2 * (FF_FIRST + 2))
                for hf in range(2):
                    pe.wait_ge(u_ready, 4 * b + (2 * hf + 2 + RING_FREE))
                    for m in range(KD):
                        q = KD * hf + m
                        o = bank[4 + q % 4][:, :]
                        pe.wait_ge(y_added, 16 * b + (q + 1))
                        for k in range(2):
                            c = k * D + m * P
                            hh, hl = u_hi[:, k, half(hf)], u_lo[:, k, half(hf)]
                            last = passes(o, w_hi[:, n2, c:c + P], w_lo[:, n2, c:c + P], hh, hl, k == 0, k == 1)
                        last.then_inc(ff2_done, 1)

            pe.sem_inc(relu_done, 4)
            pe.sem_inc(y_added, 4)
            pe.wait_ge(rms_done, SS_ATT + 2)
            for hf in range(2):
                pe.wait_ge(h_ready, ffn_number(KD - 1, hf) + 1)
                for m in range(2):
                    pe.wait_ge(main_free, MAIN_GROUPS - 1 + hf)
                    ff1(0, hf, m)
                    if hf == 1 and m == 0:
                        sum_rows(SS_FFN + 1, acc, 7)
            pe.wait_ge(rms_done, SS_FFN + 2)
            ff2(0)
            with pe.Fori(1, FF_BLOCKS) as b:
                for hf in range(2):
                    for m in range(2):
                        ff1(b, hf, m)
                ff2(b)

            pe.wait_ge(relu_done, 4 + 4 * FF_BLOCKS)

            def gate(part, i, m):
                n = GATE_FIRST + (0 if part == 0 and i == 0 else 1 + i + GATE_PIECES * part)
                q, tok, width = KD * part + 2 * i + m, tokens(part), PARTS[part][1]
                if q >= 2:
                    pe.wait_ge(gate_scaled, q - 1)
                for k in range(KD):
                    if m == 0 and k % 4 == 0:
                        pe.wait_ge(w_split, 2 * n + 1 + k // 4)
                    if i == 0 and m == 0 and part < 2:
                        pe.wait_ge(h_ready, H_PLE + KD * part + k + 1)
                    c = k * 256 + m * P
                    last = passes(bank[q % 2][:, 0:width], w_hi[:, slot(n), c:c + P], w_lo[:, slot(n), c:c + P],
                                  h_hi[:, k, tok], h_lo[:, k, tok], k == 0, k == KD - 1)
                last.then_inc(gate_done, 1)

            def project(part, m):
                q, tok, width = KD * part + m, tokens(part), PARTS[part][1]
                if q == 0:
                    pe.wait_ge(w_split, 2 * (GATE_FIRST + 1) + 2)
                if m == 0 and part < 2:
                    pe.wait_ge(pp_ready, 2 * part + 2)
                if q >= 2:
                    pe.wait_ge(x_gated, 2 * (q - 2) + 1)
                for k in range(2):
                    c = k * D + m * P
                    last = passes(bank[2 + q % 2][:, 0:width], pw_hi[:, c:c + P], pw_lo[:, c:c + P],
                                  pT_hi[:, k, tok], pT_lo[:, k, tok], k == 0, k == 1)
                last.then_inc(ple_done, 1)

            for part in range(len(PARTS)):
                for i in range(GATE_PIECES):
                    for m in range(2):
                        gate(part, i, m)
                        if part == 0 and i == 0 and m == 0:
                            pe.wait_ge(y_added, 4 + 16 * FF_BLOCKS)
                            sum_rows(SS_PLE, acc2, 4)
                    for m in range(2):
                        project(part, 2 * i + m)
                    if i == 1:
                        sum_rows(SS_PLE + 1 + part, acc2, 4)
            n = SS_FIN + LAST
            tok, width = span(n)
            pe.wait_ge(sq_used, SQ_BY[n] - 1)
            pe.wait_ge(rms_done, n)
            pe.matmul(bank[4][:, 0:width], ones[:, :], acc2[:, tok], start=True, stop=False)
            pe.wait_ge(sq_done, SQ_BY[n])
            pe.matmul(bank[4][:, 0:width], ones[:, :], ring_tile(sq2, SQ_BY[n] - 1), start=False, stop=True
                      ).then_inc(ss_done, 1)

        @block.scalar
        def _(act):
            def high(s, dst=None):
                n = s // 2
                act.wait_ge(stage_in[s % STAGES], stage_count(s))
                o = (s % 2) * HP
                hi = w_hi[:, slot(n), o:o + HP] if dst is None else dst
                act.activation(hi, stage[:, s % STAGES, :], ACT.Copy).then_inc(w_high, 1)

            def stage_count(s):
                return 16 * (s // STAGES + 1)

            def split_high(i, src, scale, k, hf):
                dst = h_hi[:, k, half(hf)]
                if H_ATT <= i < H_FFN:
                    dst = by_chunk(dst)
                if scale is None:
                    act.activation(dst, src, ACT.Copy).then_inc(h_high, 1)
                else:
                    act.activation(dst, src, ACT.Copy, scale=scale).then_inc(h_high, 1)

            def square(q, ring, src):
                if q >= RING:
                    act.wait_ge(sq_used, q - RING + 1)
                dst = ring_tile(ring, q)
                if SQ_BY[SS_LRU + 1] <= q < SQ_BY[SS_ATT + 1]:
                    dst = by_chunk(dst)
                act.activation(dst, src, ACT.Square).then_inc(sq_done, 1)

            def root(n, b, dst, width):
                act.wait_ge(ss_done, n + 1)
                tok, cols = span(n)
                act.activation(dst[:, tok], bank[b][:, 0:cols], ACT.Sqrt, bias=eps[:, 0:1],
                               scale=1.0 / width).then_inc(rms_done, 1)

            act.wait_ge(consts, 3)
            act.activation(lam[:, 2, :], ones[:, 0:LT], ACT.Square)
            act.wait_ge(first_w_in, 16)
            act.activation(w_hi[:, 0, 0:QP], stage[:, 0, 0:QP], ACT.Copy).then_inc(first_high, 1)
            act.wait_ge(vec_in, 16)
            act.wait_ge(first_x_in, 16)
            for hf in range(2):
                for k in range(KD):
                    if (k % 2 == 0) if hf or k > 1 else (k == 1):
                        act.wait_ge(x_in[4 * hf + k // 2], 16)
                    split_high(H_MIX + KD * hf + k, xT[:, k, half(hf)], v_mix[:, k:k + 1], k, hf)
                    square(KD * hf + k, sq, xT[:, k, half(hf)])
                    if hf == 0 and k == 0:
                        act.wait_ge(stage_in[0], 16)
                        act.activation(w_hi[:, 0, QP:HP], stage[:, 0, QP:HP], ACT.Copy).then_inc(w_high, 1)
                    if hf == 0 and k == 2:
                        high(1)
                    if hf == 1 and k == 3:
                        root(SS_MIX, 7, r_mix, D)
            high(2)
            high(3)
            root(SS_MIX + 1, 7, r_mix, D)
            act.wait_ge(lam_abs, 1)
            act.activation(lam[:, 1, :], lam[:, 0, :], ACT.Exp, scale=-1.0).then_inc(lam_exp, 1)

            act.wait_ge(gatew_in, 16)
            act.activation(gw_hi[:, :, :, :], gate_w[:, :, :, :], ACT.Copy).then_inc(gw_high, 1)

            def gate_input_high(j):
                act.wait_ge(conv_done, j + 1)
                for hf in range(2):
                    act.activation(gx_hi[:, half(hf)], lru_x[:, half(hf)], ACT.Copy).then_inc(gx_high, 1)

            def lru_gates(j):
                if j >= 1:
                    act.wait_ge(state_done, j)
                for hf in range(2):
                    for i, (dst, bv) in enumerate(((lru_r, v_ba), (lru_i, v_bi))):
                        act.wait_ge(gates_done, 4 * j + 2 * hf + i + 1)
                        act.activation(dst[:, half(hf)], bank[4 + 2 * hf + i][:, :], ACT.Sigmoid,
                                       bias=bv[:, j:j + 1]).then_inc(gates_sig, 1)
                act.wait_ge(lam_ready, 1)
                act.wait_ge(gates_sig, 4 * j + 4)
                act.activation(lru_u[:, :], lru_r[:, :], ACT.Tanh, scale=c_tanh[:, j:j + 1]).then_inc(lru_tanh, 1)
                act.wait_ge(lru_tanh, j + 1)
                act.activation(lru_r[:, :], lru_r[:, :], ACT.Exp, scale=c_exp[:, j:j + 1]).then_inc(lru_exp, 1)

            for g in range(IN_GROUPS):
                if g % 4 == 0 and g >= 4:
                    n = g // 4 + 1
                    piece_free(act, n - 2)
                    high(2 * n)
                    high(2 * n + 1)
                if g in GATE_AT:
                    gate_input_high(GATE_AT.index(g))
                    lru_gates(GATE_AT.index(g))
                if g - 1 in GATE_AT:
                    j = GATE_AT.index(g - 1)
                    act.wait_ge(lru_m2, j + 1)
                    act.activation(lru_u[:, :], lru_u[:, :], ACT.Sqrt).then_inc(lru_root, 1)
                if g in (15, 18):
                    for j in (2 * (g == 18), 2 * (g == 18) + 1):
                        act.wait_ge(main_free, 12 if g == 15 else 16)
                        act.activation(gl[:, j, :], gl[:, j, :], ACT.Gelu_apprx_tanh).then_inc(gelu_done, 1)
                if g in (20, 21):
                    hf = g - 20
                    act.wait_ge(state_done, LT)
                    for j in range(LT):
                        act.wait_ge(y_done, j + 1)
                        square(SQ_BY[SS_LRU + hf] - 4 + j, sq, yl[:, j, half(hf)])
                if g in (22, 23):
                    root(SS_LRU + g - 22, 5, r_lru, LRU)
                if 21 <= g < 25:
                    i = g - 21
                    act.wait_ge(vt_done, i + 1)
                    act.wait_ge(state_done, LT)
                    act.activation(v_win[:, 4 * i:4 * i + 4, :], bank[6 + i % 2][:, :].rearrange(
                        "p (c d) -> p c d", d=P), ACT.Copy).then_inc(vt_read, 1)

            def exps(u):
                act.wait_ge(max_done, u + 1)
                for i in range(8):
                    e = prob[:, u % 2, i * P:(i + 1) * P]
                    act.activation(e, e, ACT.Exp, bias=nmax[:, u % 2, i:i + 1],
                                   accum_out=den[:, u % 2, i:i + 1]).then_inc(exp_done, 1)
                act.activation(esink[:, u % 2, :], smax[:, u % 2, :], ACT.Exp).then_inc(exp_done, 1)

            def lru_high(hf):
                act.wait_ge(main_done, IN_GROUPS - 2 + 2 * hf)
                for j in range(LT):
                    act.wait_ge(y_normed, 4 * hf + j + 1)
                    split_high(H_LRU + 4 * hf + j, yl[:, j, half(hf)], None, j, hf)

            lru_high(0)
            exps(0)
            exps(1)
            lru_high(1)
            piece_free(act, 6)
            high(2 * 8)
            high(2 * 8 + 1)
            for u in range(UNITS):
                act.wait_ge(pt_done, 2 * u + 1)
                if u >= 1:
                    act.wait_ge(o_done, u)
                act.activation(probT[:, 0:512], bank[6][:, :], ACT.Copy).then_inc(pt0_read, 1)
                if u == 4:
                    piece_free(act, 7)
                    high(2 * 9)
                    high(2 * 9 + 1)
                if u + 2 < UNITS:
                    exps(u + 2)
                if u in (5, 6):
                    for j in (2 * (u - 5), 2 * (u - 5) + 1):
                        split_high(H_ATT + j, q_tile(j, 0), v_att[:, j:j + 1], LT + j, 0)
                        square(SQ_BY[SS_ATT] - 4 + j, sq, q_tile(j, 0))
            root(SS_ATT, 4, r_mix, ATT)
            act.wait_ge(o_read, UNITS)
            for j in range(LT):
                split_high(H_ATT + 4 + j, q_tile(j, 1), v_att[:, j:j + 1], LT + j, 1)
            for j in range(LT):
                square(SQ_BY[SS_ATT + 1] - 4 + j, sq, q_tile(j, 1))
            piece_free(act, 8)
            high(2 * 10)
            high(2 * 10 + 1)
            root(SS_ATT + 1, 5, r_mix, ATT)
            act.dma_start(pT[:, :, :], p.rearrange("(k q) t -> q k t", q=P)).then_inc(p_in, 16)

            def ffn_high(k, hf):
                act.wait_ge(main_free, A0 + 8 * (k // 4) + 4 * hf + k % 4 + 1)
                if k == 0:
                    act.wait_ge(main_done, A0)
                if k == 4:
                    act.wait_ge(main_done, MAIN_GROUPS - 4 + 4 * hf)
                split_high(ffn_number(k, hf), xT[:, k, half(hf)], v_ffn[:, k:k + 1], k, hf)

            def ffn_square(k, hf):
                act.wait_ge(main_free, A0 + 8 * (k // 4) + 4 * hf + k % 4 + 1)
                square(SQ_BY[SS_FFN + hf] - 8 + k, sq, xT[:, k, half(hf)])

            for k in range(4):
                ffn_square(k, 0)
                ffn_high(k, 0)
            piece_free(act, 9)
            high(2 * FF_FIRST)
            high(2 * FF_FIRST + 1)
            for k in range(4):
                ffn_high(k, 1)
            for k in range(4, KD):
                ffn_square(k, 0)
                ffn_high(k, 0)
            for k in range(4):
                ffn_square(k, 1)
            root(SS_FFN, 7, r_ffn, D)
            for k in range(4, KD):
                ffn_high(k, 1)
                ffn_square(k, 1)

            def ff_high(b, i):
                s0 = 2 * FF_FIRST + 2 + i
                n0, o = s0 // 2, (s0 % 2) * HP
                act.wait_ge(stage_in[s0 % STAGES], 16 * b + stage_count(s0))
                act.activation(w_hi[:, n0 % 2, o:o + HP], stage[:, s0 % STAGES, :], ACT.Copy).then_inc(w_high, 1)

            def ff_block(b, first):
                act.wait_ge(y_added, 16 * b + 4)
                ff_high(b, 0)
                ff_high(b, 1)
                for j in range(4):
                    hf, m = j // 2, j % 2
                    if first and j == 2:
                        root(SS_FFN + 1, 7, r_ffn, D)
                    act.wait_ge(relu_done, 4 * b + (4 + j + 1))
                    act.activation(u_hi[:, m, half(hf)], relu[:, j % 2, :], ACT.Square).then_inc(u_high, 1)
                ff_high(b, 2)
                ff_high(b, 3)

            ff_block(0, True)
            act.wait_ge(p_in, 16)
            for i in range(4):
                k, hf = i % 2, i // 2
                act.activation(pT_hi[:, k, half(hf)], pT[:, k, half(hf)], ACT.Copy).then_inc(pp_high, 1)
            with act.Fori(1, FF_BLOCKS) as b:
                ff_block(b, False)

            def ple_high(hf):
                for k in range(KD):
                    act.wait_ge(y_added, 4 + 16 * (FF_BLOCKS - 1) + KD * hf + k + 1)
                    split_high(H_PLE + KD * hf + k, xT[:, k, half(hf)], v_ple[:, k:k + 1], k, hf)
                    square(SQ_BY[SS_PLE + hf] - 8 + k, sq2, xT[:, k, half(hf)])

            def project_high():
                s0 = 2 * (GATE_FIRST + 1)
                for s in (s0, s0 + 1):
                    high(s, pw_hi[:, (s % 2) * HP:(s % 2 + 1) * HP])

            def gate_high(n):
                high(2 * n)
                high(2 * n + 1)

            ple_high(0)
            project_high()
            act.wait_ge(ff2_done, 16 * FF_BLOCKS)
            gate_high(GATE_FIRST + 2)
            root(SS_PLE, 4, r_mix, D)
            ple_high(1)

            def sigmoid(q):
                act.wait_ge(gate_scaled, q + 1)
                g = gt[:, q % 2, 0:PARTS[q // KD][1]]
                act.activation(g, g, ACT.Sigmoid).then_inc(gate_sig, 1)

            def final_square(q):
                act.wait_ge(x_gated, 2 * (q + 1))
                square(SQ_BY[SS_FIN - 1] + q, sq2, xT[:, q % KD, tokens(q // KD)])

            def final_scale(k):
                act.wait_ge(sq_done, SQ_BY[SS_FIN + LAST - 1] + k + 1)
                x_k = xT[:, k, tokens(LAST)]
                act.activation(x_k, x_k, ACT.Copy, scale=v_fin[:, k:k + 1]).then_inc(x_scaled, 1)

            for q in range(len(PARTS) * KD):
                sigmoid(q)
                if q >= 2:
                    final_square(q - 2)
                if q >= LAST * KD + 2:
                    final_scale(q - 2 - LAST * KD)
                if q % 2 == 1 and q // 2 + 2 < GATE_PIECES * len(PARTS):
                    act.wait_ge(gate_done, q + 1)
                    gate_high(GATE_FIRST + 3 + q // 2)
                if q % KD == 4:
                    root(SS_PLE + 1 + q // KD, 4, r_mix if q < KD else r_fin, D)
            for k in (KD - 2, KD - 1):
                final_square(LAST * KD + k)
                if k < KD - 1:
                    final_scale(k)
            root(SS_FIN + LAST, 4, r_fin, D)
            final_scale(KD - 1)

        @block.vector
        def _(dve):
            chained = [0]

            def link(ins):
                chained[0] += 1
                ins.then_inc(dve_chain, 1)
                dve.wait_ge(dve_chain, chained[0])

            def split_low(i, src, scale, k, hf):
                dve.wait_ge(h_high, i + 1)
                o, hi = h_lo[:, k, half(hf)], h_hi[:, k, half(hf)]
                if H_ATT <= i < H_FFN:
                    o, hi = by_chunk(o), by_chunk(hi)
                if scale is None:
                    dve.tensor_tensor(o, src, hi, ALU.subtract).then_inc(h_ready, 1)
                else:
                    dve.scalar_tensor_tensor(out=o, in0=src, scalar=scale, in1=hi, op0=ALU.mult,
                                             op1=ALU.subtract).then_inc(h_ready, 1)

            def invert(n, dst):
                dve.wait_ge(rms_done, n + 1)
                link(dve.reciprocal(dst[:, span(n)[0]], dst[:, span(n)[0]]))

            def evac(g):
                n, hf, m = g // 4, (g % 4) // 2, g % 2
                dve.wait_ge(main_done, g + 1)
                if n < 2:
                    dst = yl[:, 2 * n + m, half(hf)]
                elif n < 4:
                    dst = gl[:, 2 * (n - 2) + m, half(hf)]
                elif n == 4:
                    dst = (kT, vT)[m][:, PAD + hf * HALF:PAD + (hf + 1) * HALF]
                else:
                    dst = q_tile(2 * (n - 5) + m, hf)
                src, r = main_bank(g)[0][:, :], r_mix[:, half(hf)]
                if n >= 5:
                    src, r = by_chunk(src), by_chunk(r)
                dve.tensor_tensor(dst, src, r, ALU.mult).then_inc(main_free, 1)

            def decay():
                dve.wait_ge(lam_exp, 1)
                e, z, z2, s = lam[:, 1, :], lam[:, 2, :], lam[:, 3, :], lam[:, 0, :]
                link(dve.tensor_scalar(z, e, 2.0, None, ALU.add))
                link(dve.reciprocal(z, z))
                link(dve.tensor_tensor(z, z, e, ALU.mult))
                link(dve.tensor_tensor(z2, z, z, ALU.mult))
                link(dve.tensor_scalar(s, z2, 1.0 / 15.0, None, ALU.mult))
                for d in (13.0, 11.0, 9.0, 7.0, 5.0, 3.0):
                    link(dve.scalar_tensor_tensor(out=s, in0=s, scalar=1.0 / d, in1=z2, op0=ALU.add, op1=ALU.mult))
                link(dve.scalar_tensor_tensor(out=s, in0=s, scalar=1.0, in1=z, op0=ALU.add, op1=ALU.mult))
                link(dve.tensor_scalar(e, v_lam, -1.0, 0.0, ALU.mult, ALU.max))
                link(dve.scalar_tensor_tensor(out=s, in0=s, scalar=2.0, in1=e, op0=ALU.mult, op1=ALU.add))
                dve.tensor_scalar(c_tanh, s, 4.0, None, ALU.mult).then_inc(dve_chain, 1)
                chained[0] += 1
                dve.wait_ge(dve_chain, chained[0])
                dve.tensor_scalar(c_exp, s, -8.0, None, ALU.mult).then_inc(lam_ready, 1)

            def conv(j):
                dve.wait_ge(main_free, 4 if j < 2 else 8)
                if j >= 1:
                    dve.wait_ge(state_done, j)
                link(dve.tensor_scalar(lru_x[:, :], yl[:, j, :], v_conv[:, 12 + j:13 + j], v_bconv[:, j:j + 1],
                                       ALU.mult, ALU.add))
                for s in (1, 2, 3):
                    c = 4 * (3 - s) + j
                    ins = dve.scalar_tensor_tensor(out=lru_x[:, s:], in0=yl[:, j, 0:SEQ - s],
                                                   scalar=v_conv[:, c:c + 1], in1=lru_x[:, s:],
                                                   op0=ALU.mult, op1=ALU.add)
                    if s < 3:
                        link(ins)
                    else:
                        ins.then_inc(conv_done, 1)

            def decays(j):
                dve.wait_ge(lru_exp, j + 1)
                link(dve.scalar_tensor_tensor(out=lru_u[:, :], in0=lru_r[:, :], scalar=1.0, in1=lru_u[:, :],
                                              op0=ALU.add, op1=ALU.mult))
                link(dve.tensor_scalar(lru_r[:, :], lru_u[:, :], -1.0, 1.0, ALU.mult, ALU.add))
                link(dve.scalar_tensor_tensor(out=lru_u[:, :], in0=lru_r[:, :], scalar=1.0, in1=lru_u[:, :],
                                              op0=ALU.add, op1=ALU.mult))
                dve.tensor_scalar(lru_u[:, :], lru_u[:, :], 1e-34, None, ALU.max).then_inc(lru_m2, 1)
                dve.wait_ge(conv_done, j + 1)
                link(dve.tensor_tensor(lru_x[:, :], lru_i[:, :], lru_x[:, :], ALU.mult))

            def states(j):
                dve.wait_ge(lru_root, j + 1)
                link(dve.tensor_tensor(lru_x[:, :], lru_x[:, :], lru_u[:, :], ALU.mult))
                dve.tensor_tensor_scan(yl[:, j, :], lru_r[:, :], lru_x[:, :], 0.0, ALU.mult, ALU.add
                                       ).then_inc(state_done, 1)

            dve.memset(kT[:, 0:PAD], 0.0).then_inc(pads_ready, 1)
            dve.memset(vT[:, 0:PAD], 0.0).then_inc(pads_ready, 1)
            dve.wait_ge(first_high, 1)
            dve.tensor_tensor(w_lo[:, 0, 0:QP], stage[:, 0, 0:QP], w_hi[:, 0, 0:QP], ALU.subtract
                              ).then_inc(first_low, 1)
            dve.wait_ge(vec_in, 16)
            for k in range(KD):
                split_low(H_MIX + k, xT[:, k, half(0)], v_mix[:, k:k + 1], k, 0)
                add_square(dve, SS_MIX, k, sq, acc)
                if k == 0:
                    dve.wait_ge(w_high, 1)
                    dve.tensor_tensor(w_lo[:, 0, QP:HP], stage[:, 0, QP:HP], w_hi[:, 0, QP:HP], ALU.subtract
                                      ).then_inc(w_split, 1)
            dve.scalar_tensor_tensor(out=lam[:, 0, :], in0=v_lam, scalar=-1.0, in1=v_lam, op0=ALU.mult,
                                     op1=ALU.max).then_inc(lam_abs, 1)
            link(dve.tensor_scalar(nsink[:, :], sink, -1.0, None, ALU.mult))
            for k in range(KD):
                split_low(H_MIX + KD + k, xT[:, k, half(1)], v_mix[:, k:k + 1], k, 1)
                if k < 2:
                    add_square(dve, SS_MIX + 1, k, sq, acc)
            invert(SS_MIX, r_mix)
            evac(0)
            evac(1)
            invert(SS_MIX + 1, r_mix)
            evac(2)
            evac(3)
            conv(0)
            decay()

            def multiply_y(j):
                dve.wait_ge(gelu_done, j + 1)
                dve.wait_ge(state_done, j + 1)
                dve.tensor_tensor(yl[:, j, :], yl[:, j, :], gl[:, j, :], ALU.mult).then_inc(y_done, 1)

            def norm_y(hf):
                for j in range(LT):
                    dve.wait_ge(sq_done, SQ_BY[SS_LRU + hf] - 3 + j)
                    dve.scalar_tensor_tensor(out=yl[:, j, half(hf)], in0=yl[:, j, half(hf)],
                                             scalar=v_lru[:, j:j + 1], in1=r_lru[:, half(hf)],
                                             op0=ALU.mult, op1=ALU.mult).then_inc(y_normed, 1)

            def low_y(hf):
                for j in range(LT):
                    dve.wait_ge(y_normed, 4 * hf + j + 1)
                    split_low(H_LRU + 4 * hf + j, yl[:, j, half(hf)], None, j, hf)

            def softmax_front(u):
                if u >= 2:
                    dve.wait_ge(pt_done, 2 * (u - 1))
                s = prob[:, u % 2, :]
                for g in range(NKV):
                    dve.wait_ge(s_done, 2 * u + g + 1)
                    dve.scalar_tensor_tensor(
                        out=s[:, g * 512:(g + 1) * 512].rearrange("p (c k) -> p c k", c=2),
                        in0=bank[4 + g][:, :].rearrange("p (c k) -> p c k", c=2), scalar=HD ** -0.5,
                        in1=bias[:, g * 256:(g + 1) * 256].unsqueeze(1).to_broadcast([P, 2, 256]),
                        op0=ALU.mult, op1=ALU.add).then_inc(s_read, 1)
                dve.wait_ge(s_read, 2 * u + 2)
                blocks = s.rearrange("p (b k) -> p b k", k=P)
                if u == 0:
                    for g in range(NKV):
                        link(dve.memset(s[:, g * 512:g * 512 + 256].rearrange("p (a k) -> p a k", a=2)[:, :, 0:PAD],
                                        NEG_INF))
                nm, sm = nmax[:, u % 2, :], smax[:, u % 2, :]
                link(dve.tensor_reduce(nm, blocks, AX.X, ALU.max))
                link(dve.scalar_tensor_tensor(out=nm, in0=nm, scalar=-1.0, in1=nsink[:, :], op0=ALU.mult,
                                              op1=ALU.min))
                dve.tensor_tensor(sm, sink, nm, ALU.add).then_inc(max_done, 1)

            def softmax_sum(u):
                dve.wait_ge(exp_done, 9 * (u + 1))
                d = den[:, u % 2, :]
                link(dve.tensor_tensor(d, d, esink[:, u % 2, :], ALU.add))
                dve.reciprocal(d, d).then_inc(den_done, 1)

            def read_o(u):
                dve.wait_ge(o_done, u + 1)
                dve.tensor_copy(qT[:, 2 * u:2 * u + 2, :, :],
                                bank[3][:, :].rearrange("p (c j q) -> p c j q", c=2, q=CHUNK)).then_inc(o_read, 1)

            def add_l(g):
                n, hf, m = g // 8, (g % 8) // 4, g % 4
                dve.wait_ge(main_done, L0 + g + 1)
                dst = xT[:, 4 * n + m, half(hf)]
                dve.tensor_tensor(dst, main_bank(L0 + g)[0][:, :], dst, ALU.add).then_inc(main_free, 1)

            for g in range(4, IN_GROUPS - 2):
                if g + 1 in GATE_AT[1:]:
                    conv(GATE_AT.index(g + 1))
                evac(g)
                if g - 1 in GATE_AT:
                    decays(GATE_AT.index(g - 1))
                if g - 2 in GATE_AT:
                    states(GATE_AT.index(g - 2))
                if g == 17:
                    multiply_y(0)
                    multiply_y(1)
                if g == 20:
                    multiply_y(2)
                    multiply_y(3)
                if g == 24:
                    invert(SS_LRU, r_lru)
                    norm_y(0)
            low_y(0)
            dve.wait_ge(bias_in, 16)
            dve.wait_ge(y_done, LT)
            softmax_front(0)
            invert(SS_LRU + 1, r_lru)
            softmax_sum(0)
            softmax_front(1)
            norm_y(1)
            evac(IN_GROUPS - 2)
            evac(IN_GROUPS - 1)
            softmax_sum(1)
            low_y(1)
            for u in range(UNITS):
                if u >= 1:
                    read_o(u - 1)
                if 1 <= u < UNITS - 1:
                    softmax_sum(u + 1)
                add_l(2 * u)
                dve.wait_ge(pt_done, 2 * u + 2)
                if u >= 1:
                    dve.wait_ge(o_done, u)
                dve.tensor_copy(probT[:, 512:1024], bank[7][:, :]).then_inc(pt1_read, 1)
                if u + 2 < UNITS:
                    softmax_front(u + 2)
                add_l(2 * u + 1)
                if u == 6:
                    for j in range(LT):
                        split_low(H_ATT + j, q_tile(j, 0), v_att[:, j:j + 1], LT + j, 0)
                        add_square(dve, SS_ATT, j, sq, acc)
            invert(SS_ATT, r_mix)
            read_o(UNITS - 1)
            for j in range(LT):
                split_low(H_ATT + 4 + j, q_tile(j, 1), v_att[:, j:j + 1], LT + j, 1)

            def add_a(g):
                n, hf, m = g // 8, (g % 8) // 4, g % 4
                dve.wait_ge(main_done, A0 + g + 1)
                s = scaled[:, g % 2, :]
                link(dve.tensor_tensor(s, main_bank(A0 + g)[0][:, :], r_mix[:, half(hf)], ALU.mult))
                dst = xT[:, 4 * n + m, half(hf)]
                dve.tensor_tensor(dst, dst, s, ALU.add).then_inc(main_free, 1)

            def ffn_low(k, hf):
                split_low(ffn_number(k, hf), xT[:, k, half(hf)], v_ffn[:, k:k + 1], k, hf)

            add_a(0)
            for j in range(LT):
                add_square(dve, SS_ATT + 1, j, sq, acc)
            for g in range(1, 4):
                add_a(g)
            invert(SS_ATT + 1, r_mix)
            for g in range(4, A_GROUPS):
                if g < 8:
                    ffn_low(g - 4, 0)
                elif g < 12:
                    ffn_low(g - 8, 1)
                else:
                    ffn_low(g - 8, 0)
                add_a(g)
            for k in range(4, KD):
                ffn_low(k, 1)
            invert(SS_FFN, r_ffn)

            dve.sem_inc(u_sq, RING_FREE)
            dve.sem_inc(u_ready, RING_FREE)
            dve.sem_inc(u_high, RING_FREE)

            def hidden(b, j):
                hf, m = j // 2, j % 2
                dve.wait_ge(ff1_done, 4 * b + (j + 1))
                dve.wait_ge(u_high, 4 * b + (j - 1 + RING_FREE))
                dve.wait_ge(u_sq, 4 * b + (j - 1 + RING_FREE))
                dve.scalar_tensor_tensor(out=relu[:, j % 2, :], in0=bank[j][:, :], scalar=0.0,
                                         in1=r_ffn[:, half(hf)], op0=ALU.max, op1=ALU.mult).then_inc(relu_done, 1)
                dve.wait_ge(relu_done, 4 * b + (4 + j + 1))
                dve.wait_ge(u_ready, 4 * b + (j - 1 + RING_FREE))
                dve.tensor_tensor(usq[:, j % 2, :], relu[:, j % 2, :], relu[:, j % 2, :], ALU.mult
                                  ).then_inc(u_sq, 1)
                dve.wait_ge(u_sq, 4 * b + (RING_FREE + j + 1))
                dve.wait_ge(u_high, 4 * b + (RING_FREE + j + 1))
                dve.tensor_tensor(u_lo[:, m, half(hf)], usq[:, j % 2, :], u_hi[:, m, half(hf)],
                                  ALU.subtract).then_inc(u_ready, 1)

            def add_ff(b, q):
                hf, m = q // KD, q % KD
                dve.wait_ge(ff2_done, 16 * b + (q + 1))
                dst = xT[:, m, half(hf)]
                dve.tensor_tensor(dst, bank[4 + q % 4][:, :], dst, ALU.add).then_inc(y_added, 1)

            for j in range(4):
                if j == 2:
                    invert(SS_FFN + 1, r_ffn)
                hidden(0, j)
            for q in range(16):
                add_ff(0, q)
                if q >= 12:
                    i = q - 12
                    k, hf = i % 2, i // 2
                    dve.wait_ge(pp_high, i + 1)
                    dve.tensor_tensor(pT_lo[:, k, half(hf)], pT[:, k, half(hf)], pT_hi[:, k, half(hf)],
                                      ALU.subtract).then_inc(pp_ready, 1)
            with dve.Fori(1, FF_BLOCKS - 1) as b:
                for j in range(4):
                    hidden(b, j)
                for q in range(16):
                    add_ff(b, q)
            for j in range(4):
                hidden(FF_BLOCKS - 1, j)
            for q in range(16):
                add_ff(FF_BLOCKS - 1, q)
                if q >= KD:
                    k = q - KD
                    split_low(H_PLE + k, xT[:, k, half(0)], v_ple[:, k:k + 1], k, 0)
            invert(SS_PLE, r_mix)

            def gate_scale(q):
                part, width = q // KD, PARTS[q // KD][1]
                dve.wait_ge(gate_done, q + 1)
                if q >= 2:
                    dve.wait_ge(x_gated, 2 * (q - 1))
                dve.tensor_tensor(gt[:, q % 2, 0:width], bank[q % 2][:, 0:width], r_mix[:, tokens(part)], ALU.mult
                                  ).then_inc(gate_scaled, 1)

            def gate_add(q):
                width, x_q = PARTS[q // KD][1], xT[:, q % KD, tokens(q // KD)]
                g = gt[:, q % 2, 0:width]
                dve.wait_ge(gate_sig, q + 1)
                dve.wait_ge(ple_done, q + 1)
                dve.tensor_tensor(g, bank[2 + q % 2][:, 0:width], g, ALU.mult).then_inc(x_gated, 1)
                dve.wait_ge(x_gated, 2 * q + 1)
                dve.tensor_tensor(x_q, x_q, g, ALU.add).then_inc(x_gated, 1)

            def out_tile(k, part):
                if part > 0:
                    dve.wait_ge(out_done[k // 2], 16)
                dve.scalar_tensor_tensor(out=result(k, part), in0=xT[:, k, tokens(part)], scalar=v_fin[:, k:k + 1],
                                         in1=r_fin[:, tokens(part)], op0=ALU.mult, op1=ALU.mult
                                         ).then_inc(out_ready[k], 1)

            for q in range(len(PARTS) * KD):
                part, k = q // KD, q % KD
                gate_scale(q)
                if q == 0:
                    for i in range(KD):
                        split_low(H_PLE + KD + i, xT[:, i, half(1)], v_ple[:, i:i + 1], i, 1)
                if k % 2 == 1:
                    gate_add(q - 1)
                    gate_add(q)
                if k == 5:
                    invert(SS_PLE + 1 + part, r_mix if part == 0 else r_fin)
                for i, before in OUT_AT.get(q, ()):
                    out_tile(i, before)

            dve.wait_ge(rms_done, SS_FIN + LAST + 1)
            r_last = r_fin[:, tokens(LAST)]
            dve.reciprocal(r_last, r_last).then_inc(fin_ready, 1)
            dve.wait_ge(fin_ready, 1)
            dve.wait_ge(x_scaled, KD)
            for k in DVE_OUT:
                dve.wait_ge(out_done[k // 2], 16)
                dve.tensor_tensor(result(k, LAST), xT[:, k, tokens(LAST)], r_last, ALU.mult
                                  ).then_inc(out_ready[k], 1)


def kernel(**inputs):
    import concourse.bacc as bacc
    from concourse.bass_utils import run_bass_kernel_spmd

    f = {n: np.asarray(a) for n, a in inputs.items()}

    def pieces(w, kt):
        rows, cols = w.shape
        c = PIECE // kt
        w = w.reshape(rows // (kt * P), 2, kt // 2, P, cols // c, c)
        return np.ascontiguousarray(w.transpose(0, 4, 1, 3, 2, 5).reshape(-1, 2, P, HP))

    heads = np.arange(ATT).reshape(NKV, NQ // NKV, HD).transpose(1, 0, 2).ravel()
    w_in = f["w_in"][0]
    o2, o3 = 2 * LRU, 2 * LRU + ATT
    w_in = np.concatenate([w_in[:, :o2], w_in[:, o3:], w_in[:, o2:o3][:, heads]], axis=1)
    w_out = np.concatenate([f["w_out"][0][:LRU], f["w_out"][0][LRU:][heads]], axis=0)
    gates_w = np.zeros((P, 2, LT, P), np.float32)
    for i, n in enumerate(("w_lru_a", "w_lru_i")):
        for j in range(LT):
            for b in range(2):
                gates_w[b * HD:(b + 1) * HD, i, j, b * HD:(b + 1) * HD] = f[n][0, 2 * j + b]
    sinks = f["sinks"][0].reshape(NKV, 1, 2, 2).repeat(2, axis=1).transpose(3, 0, 1, 2).reshape(2, 1, 8).repeat(
        HD, axis=1).reshape(P, 8)
    columns = {n: f[n].reshape(-1, P).T for n in VEC if n != "sinks"}
    columns["g_attn_out"] = f["g_attn_out"][0][heads].reshape(-1, P).T
    columns["sinks"] = sinks
    arrays = {
        "x": np.ascontiguousarray(f["x"][0].T),
        "p": np.ascontiguousarray(f["p"][0, 0].T),
        "vectors": np.ascontiguousarray(np.concatenate([columns[n] for n in VEC], axis=1)),
        "gates_w": gates_w,
        "w_in": pieces(w_in, KD),
        "w_out": pieces(w_out, LT),
        "w_ff1": pieces(f["w_ff1"][0], KD),
        "w_ff2": pieces(f["w_ff2"][0], 2),
        "w_ple_gate": pieces(f["w_ple_gate"][0], KD),
        "w_ple_proj": pieces(f["w_ple_proj"][0], 2),
    }
    head = (4 * np.arange(2)[None, :, None] + 2 * np.arange(2)[None, None, :]
            + np.repeat(np.arange(2), HD)[:, None, None])
    dist = np.abs(CHUNK + np.tile(np.arange(CHUNK), 2)[:, None] - np.arange(2 * CHUNK)[None, :])
    arrays["alibi"] = (-(2.0 ** -(head + 1.0))[:, :, :, None] * dist[:, None, None, :]).reshape(P, 512).astype(
        np.float32)
    nc = bacc.Bacc("TRN2", target_bir_lowering=False, num_devices=1, dynamic_dma_scratch_size=1024)
    args = {n: nc.dram_tensor(f"in_{n}", a.shape, mybir.dt.from_np(a.dtype), kind="ExternalInput").ap()
            for n, a in arrays.items()}
    out = nc.dram_tensor("out_x", (D, SEQ), F32, kind="ExternalOutput").ap()
    build(nc, out=out, **args)
    r = run_bass_kernel_spmd(nc, [{f"in_{n}": a for n, a in arrays.items()}], core_ids=[0])
    return np.ascontiguousarray(r.results[0]["out_x"].T).reshape(1, SEQ, D)
```
